# Optimizing a Trainium2 kernel written in Bass

```python
import jax, jax.numpy as jnp
from jax import lax
import numpy as np

D_MODEL = 1024
BATCH = 1
SEQ = 256
DEPTH = 1
DEC_BATCH = 8
DEC_SEQ = 1
PAST_LEN = 1024
PAGE_SIZE = 128

N_META = 16
H_A = 4
DK_A = 128
DV_A = 128
CONV_W = 4
CHUNK = 64
H_F = 8
HD_F = 64
Q_BLOCK = 128
N_EXP = 32
TOP_K = 4
D_EXP = D_MODEL
SWIGLU_LIMIT = 7.0
SWIGLU_ALPHA = 1.702
MOE_BLOCK = 128
EPS = 1e-6

QK_A = H_A * DK_A
VW_A = H_A * DV_A
QKV_A = 2 * QK_A + VW_A
W_F = H_F * HD_F
IN_COLS = (QKV_A, VW_A, H_A, H_A, W_F, W_F, W_F, H_F, D_MODEL, D_MODEL)
D_IN = sum(IN_COLS)

kernel_name = 'hybrid_gdn_fox_moe_step'

def _rmsnorm(x, g):
    xf = x.astype(jnp.float32)
    return xf * lax.rsqrt(jnp.mean(xf * xf, axis=-1, keepdims=True) + EPS) * g.astype(jnp.float32)

def _l2norm(x):
    return x * lax.rsqrt(jnp.sum(x * x, axis=-1, keepdims=True) + EPS)

def _split_cols(a):
    out, s = [], 0
    for w in IN_COLS:
        out.append(a[..., s:s + w])
        s += w
    return out

def _causal_conv(x_ext, w):
    c = x_ext.shape[-1]
    return lax.conv_general_dilated(x_ext, w.astype(jnp.float32)[:, None, :], (1,), 'VALID',
                                    dimension_numbers=('NWC', 'WIO', 'NWC'), feature_group_count=c)

def _delta_chunk(S, q, k, v, beta, g):
    C = q.shape[2]
    G = jnp.cumsum(g, axis=-1)
    incl = jnp.tril(jnp.ones((C, C), bool))
    strict = jnp.tril(jnp.ones((C, C), bool), -1)
    decay = jnp.exp(jnp.where(incl, G[..., :, None] - G[..., None, :], -jnp.inf))
    eG = jnp.exp(G)
    A = jnp.where(strict, beta[..., :, None] * decay * jnp.einsum('bhid,bhjd->bhij', k, k), 0.0)
    rhs = beta[..., None] * (v - eG[..., None] * jnp.einsum('bhid,bhdv->bhiv', k, S))
    delta = lax.linalg.triangular_solve(A + jnp.eye(C, dtype=A.dtype), rhs, left_side=True, lower=True)
    o = (eG[..., None] * jnp.einsum('bhid,bhdv->bhiv', q, S)
         + jnp.einsum('bhij,bhjv->bhiv', jnp.einsum('bhid,bhjd->bhij', q, k) * decay, delta))
    g_end = G[..., -1:]
    S_new = (jnp.exp(g_end)[..., None] * S
             + jnp.einsum('bhjd,bhjv->bhdv', k * jnp.exp(g_end - G)[..., None], delta))
    return S_new, o

def _delta_scan(S0, q, k, v, beta, g, chunk):
    B, H, T = beta.shape
    n = T // chunk

    def blocks(a):
        return jnp.moveaxis(a.reshape((B, H, n, chunk) + a.shape[3:]), 2, 0)

    S, o = lax.scan(lambda s, inp: _delta_chunk(s, *inp), S0,
                    tuple(blocks(a) for a in (q, k, v, beta, g)))
    return S, jnp.moveaxis(o, 0, 2).reshape(B, H, T, -1)

def _forgetting_attention(q, k, v, c_q, c_k, q_pos, k_pos):
    B, T, H, d = q.shape
    qb = min(Q_BLOCK, T)
    nb = -(-T // qb)
    pad = nb * qb - T
    scale = d ** -0.5
    qp = jnp.pad(q, ((0, 0), (0, pad), (0, 0), (0, 0))).reshape(B, nb, qb, H, d).swapaxes(0, 1)
    cp = jnp.pad(c_q, ((0, 0), (0, pad), (0, 0))).reshape(B, nb, qb, H).swapaxes(0, 1)
    pp = jnp.pad(q_pos, (0, pad), mode='edge').reshape(nb, qb)
    c_kT = jnp.swapaxes(c_k, 1, 2)

    def block(args):
        qi, ci, pi = args
        s = (jnp.einsum('bqhd,bkhd->bhqk', qi, k) * scale
             + (jnp.swapaxes(ci, 1, 2)[..., None] - c_kT[:, :, None, :]))
        s = jnp.where(k_pos[None, :] <= pi[:, None], s, -jnp.inf)
        p = jax.nn.softmax(s, axis=-1)
        return jnp.einsum('bhqk,bkhd->bqhd', p, v)

    o = lax.map(block, (qp, cp, pp))
    return o.swapaxes(0, 1).reshape(B, nb * qb, H, d)[:, :T]

def _moe(h, w_router, b_router, w_gate, b_gate, w_up, b_up, w_down, b_down):
    n_tok, dm = h.shape
    logits = (h @ w_router + b_router).astype(jnp.float32)
    top_val, top_idx = lax.top_k(logits, TOP_K)
    top_w = jax.nn.softmax(top_val, axis=-1)
    m = n_tok * TOP_K
    bm = min(MOE_BLOCK, -(-m // 8) * 8)
    n_blk = -(-(m + N_EXP * (bm - 1)) // bm)
    flat_e = top_idx.reshape(-1)
    order = jnp.argsort(flat_e)
    e_s = flat_e[order]
    tok_s = (order // TOP_K).astype(jnp.int32)
    w_s = top_w.reshape(-1)[order]
    counts = jnp.zeros((N_EXP,), jnp.int32).at[flat_e].add(1)
    padded = (counts + bm - 1) // bm * bm
    start = jnp.cumsum(counts) - counts
    pstart = jnp.cumsum(padded) - padded
    dest = pstart[e_s] + jnp.arange(m) - start[e_s]
    row_tok = jnp.full((n_blk * bm,), n_tok, jnp.int32).at[dest].set(tok_s)
    h_ext = jnp.concatenate([h, jnp.zeros((1, dm), h.dtype)], axis=0)
    xb = h_ext[row_tok].reshape(n_blk, bm, dm)
    blk_e = jnp.minimum(jnp.searchsorted(jnp.cumsum(padded), jnp.arange(n_blk) * bm, side='right'), N_EXP - 1)

    def expert(args):
        xi, e = args
        gate = jnp.minimum(xi @ w_gate[e] + b_gate[e], SWIGLU_LIMIT)
        up = jnp.clip(xi @ w_up[e] + b_up[e], -SWIGLU_LIMIT, SWIGLU_LIMIT)
        return ((up + 1.0) * gate * jax.nn.sigmoid(SWIGLU_ALPHA * gate)) @ w_down[e] + b_down[e]

    y = lax.map(expert, (xb, blk_e)).reshape(n_blk * bm, dm)
    return jax.ops.segment_sum(y[dest] * w_s[:, None], tok_s, num_segments=n_tok)

def _layer(x, conv_prev, S0, k_past, v_past, lf_past, lead_pad, chunk,
           g_mix, w_in, conv_w, a_log, dt_bias, norm_a, qn_g, kn_g, b_forget, p_a, p_f, w_o,
           g_ffn, w_router, b_router, w_gate, b_gate, w_up, b_up, w_down, b_down):
    f32 = jnp.float32
    B, T, _ = x.shape
    h = _rmsnorm(x, g_mix)
    (qkv_a, z_a, b_a, a_a, q_f, k_f, v_f, f_f, gate_a, gate_f) = _split_cols(
        jnp.einsum('btd,de->bte', h, w_in))

    x_ext = jnp.concatenate([conv_prev.astype(f32), qkv_a.astype(f32)], axis=1)
    conv_new = x_ext[:, -(CONV_W - 1):]
    qkv = jax.nn.silu(_causal_conv(x_ext, conv_w))
    qa = _l2norm(qkv[..., :QK_A].reshape(B, T, H_A, DK_A)) * DK_A ** -0.5
    ka = _l2norm(qkv[..., QK_A:2 * QK_A].reshape(B, T, H_A, DK_A))
    va = qkv[..., 2 * QK_A:].reshape(B, T, H_A, DV_A)
    beta = jax.nn.sigmoid(b_a.astype(f32))
    g = -jnp.exp(a_log.astype(f32)) * jax.nn.softplus(a_a.astype(f32) + dt_bias)

    def to_bh(a):
        a = jnp.moveaxis(a, 1, 2)
        return jnp.pad(a, [(0, 0), (0, 0), (lead_pad, 0)] + [(0, 0)] * (a.ndim - 3))

    S_new, o = _delta_scan(S0.astype(f32), *(to_bh(a) for a in (qa, ka, va, beta, g)), chunk)
    o = jnp.moveaxis(o[:, :, lead_pad:], 1, 2)
    o_a = (_rmsnorm(o, norm_a) * jax.nn.silu(z_a.astype(f32).reshape(B, T, H_A, DV_A))).reshape(B, T, VW_A)

    qf = _rmsnorm(q_f.reshape(B, T, H_F, HD_F), qn_g)
    kf = _rmsnorm(k_f.reshape(B, T, H_F, HD_F), kn_g)
    vf = v_f.astype(f32).reshape(B, T, H_F, HD_F)
    lf = jax.nn.log_sigmoid(f_f.astype(f32) + b_forget)
    if k_past is None:
        k_all, v_all, lf_all = kf, vf, lf
    else:
        k_all = jnp.concatenate([k_past.astype(f32), kf], axis=1)
        v_all = jnp.concatenate([v_past.astype(f32), vf], axis=1)
        lf_all = jnp.concatenate([lf_past.astype(f32), lf], axis=1)
    P = k_all.shape[1] - T
    c = jnp.cumsum(lf_all, axis=1)
    o_f = _forgetting_attention(qf, k_all, v_all, c[:, P:], c,
                                P + jnp.arange(T), jnp.arange(P + T)).reshape(B, T, W_F)

    mixed = jax.nn.sigmoid(gate_a) * (o_a @ p_a) + jax.nn.sigmoid(gate_f) * (o_f @ p_f)
    x = x + mixed @ w_o
    y = _moe(_rmsnorm(x, g_ffn).reshape(B * T, D_MODEL), w_router, b_router,
             w_gate, b_gate, w_up, b_up, w_down, b_down)
    x = x + y.reshape(B, T, D_MODEL)
    return x, (kf, vf, lf, S_new, conv_new)

def setup_inputs(seed: int = 0) -> dict:
    key = jax.random.key(seed)
    ks = iter(jax.random.split(key, 40))

    def nrm(shape, scale):
        return jax.random.normal(next(ks), shape, jnp.float32) * scale

    L = DEPTH
    n_pages = PAST_LEN // PAGE_SIZE
    n_used = DEC_BATCH * n_pages
    n_pool = n_used + n_used // 4
    page_table = jax.random.permutation(next(ks), n_pool)[:n_used].reshape(DEC_BATCH, n_pages).astype(jnp.int32)
    dt = jnp.exp(jax.random.uniform(next(ks), (L, H_A), jnp.float32, minval=np.log(1e-3), maxval=np.log(1e-1)))
    return dict(
        x_prompt=nrm((BATCH, SEQ, D_MODEL), 1.0),
        x_sample=nrm((DEC_BATCH, DEC_SEQ, D_MODEL), 1.0),
        cache_k=nrm((L, n_pool, PAGE_SIZE, H_F, HD_F), 1.0),
        cache_v=nrm((L, n_pool, PAGE_SIZE, H_F, HD_F), 1.0),
        cache_logf=jax.nn.log_sigmoid(2.0 + nrm((L, n_pool, PAGE_SIZE, H_F), 0.5)),
        state_delta=nrm((L, DEC_BATCH, H_A, DK_A, DV_A), DK_A ** -0.5),
        state_conv=nrm((L, DEC_BATCH, CONV_W - 1, QKV_A), 1.0),
        page_table=page_table,
        meta_tokens=nrm((N_META, D_MODEL), 1.0),
        g_mix=1.0 + nrm((L, D_MODEL), 0.02),
        w_in=nrm((L, D_MODEL, D_IN), D_MODEL ** -0.5),
        conv_w=nrm((L, CONV_W, QKV_A), CONV_W ** -0.5),
        a_log=jnp.log(jax.random.uniform(next(ks), (L, H_A), jnp.float32, minval=1.0, maxval=16.0)),
        dt_bias=dt + jnp.log(-jnp.expm1(-dt)),
        norm_a=1.0 + nrm((L, DV_A), 0.02),
        qn_g=1.0 + nrm((L, HD_F), 0.02),
        kn_g=1.0 + nrm((L, HD_F), 0.02),
        b_forget=2.0 + nrm((L, H_F), 0.5),
        p_a=nrm((L, VW_A, D_MODEL), VW_A ** -0.5),
        p_f=nrm((L, W_F, D_MODEL), W_F ** -0.5),
        w_o=nrm((L, D_MODEL, D_MODEL), D_MODEL ** -0.5),
        g_ffn=1.0 + nrm((L, D_MODEL), 0.02),
        w_router=nrm((L, D_MODEL, N_EXP), D_MODEL ** -0.5),
        b_router=nrm((L, N_EXP), 0.01),
        w_gate=nrm((L, N_EXP, D_MODEL, D_EXP), D_MODEL ** -0.5),
        b_gate=nrm((L, N_EXP, D_EXP), 0.01),
        w_up=nrm((L, N_EXP, D_MODEL, D_EXP), D_MODEL ** -0.5),
        b_up=nrm((L, N_EXP, D_EXP), 0.01),
        w_down=nrm((L, N_EXP, D_EXP, D_MODEL), D_EXP ** -0.5),
        b_down=nrm((L, N_EXP, D_MODEL), 0.01),
    )

def reference(x_prompt, x_sample, cache_k, cache_v, cache_logf, state_delta, state_conv, page_table,
              meta_tokens, g_mix, w_in, conv_w, a_log, dt_bias, norm_a, qn_g, kn_g, b_forget,
              p_a, p_f, w_o, g_ffn, w_router, b_router, w_gate, b_gate, w_up, b_up, w_down, b_down):
    B = x_prompt.shape[0]
    Bd = x_sample.shape[0]
    xp = jnp.concatenate([jnp.broadcast_to(meta_tokens.astype(x_prompt.dtype)[None], (B, N_META, D_MODEL)),
                          x_prompt], axis=1)
    xs = x_sample
    lead_pad = (-N_META) % CHUNK
    new_p = [[] for _ in range(5)]
    new_s = [[] for _ in range(5)]
    for l in range(DEPTH):
        w = (g_mix[l], w_in[l], conv_w[l], a_log[l], dt_bias[l], norm_a[l], qn_g[l], kn_g[l], b_forget[l],
             p_a[l], p_f[l], w_o[l], g_ffn[l], w_router[l], b_router[l], w_gate[l], b_gate[l],
             w_up[l], b_up[l], w_down[l], b_down[l])
        conv0 = jnp.zeros((B, CONV_W - 1, QKV_A), jnp.float32)
        S0 = jnp.zeros((B, H_A, DK_A, DV_A), jnp.float32)
        xp, st_p = _layer(xp, conv0, S0, None, None, None, lead_pad, CHUNK, *w)
        k_past = cache_k[l][page_table].reshape(Bd, -1, H_F, HD_F)
        v_past = cache_v[l][page_table].reshape(Bd, -1, H_F, HD_F)
        lf_past = cache_logf[l][page_table].reshape(Bd, -1, H_F)
        xs, st_s = _layer(xs, state_conv[l], state_delta[l], k_past, v_past, lf_past, 0, xs.shape[1], *w)
        for lst, a in zip(new_p, st_p):
            lst.append(a)
        for lst, a in zip(new_s, st_s):
            lst.append(a)
    k_p, v_p, lf_p, d_p, c_p = (jnp.stack(a) for a in new_p)
    k_s, v_s, lf_s, d_s, c_s = (jnp.stack(a) for a in new_s)
    return (xp[:, N_META:], xs, k_p, v_p, lf_p, k_s, v_s, lf_s, d_p, d_s, c_p, c_s)


_drawn_inputs = setup_inputs


def setup_inputs(seed=0):
    import zlib

    import numpy as np

    out = dict(_drawn_inputs(seed))
    spreads = {}
    factors = {'qn_g': 3.331,
     'b_gate': 8.0,
     'b_up': 23.435,
     'b_down': 8.0,
     'norm_a': 2.672,
     'b_router': 3.218}
    for name, (base, spread) in spreads.items():
        noise = np.random.default_rng([zlib.crc32(name.encode()), seed]).standard_normal(out[name].shape)
        drawn = base * np.exp(spread * noise) if base else spread * noise
        out[name] = __import__('jax').numpy.asarray(drawn.astype(out[name].dtype))
    for name, factor in factors.items():
        out[name] = (out[name] * factor).astype(out[name].dtype)
    return out
```

```python
import concourse.bass as bass
from concourse import mybir
from contextlib import ExitStack

F32 = mybir.dt.float32
I32 = mybir.dt.int32
U32 = mybir.dt.uint32
ALU = mybir.AluOpType
ACT = mybir.ActivationFunctionType
AX = mybir.AxisListType

P = 128
D = 1024
KT = D // P
NP = 272
NS = 8
NMETA = 16
T = NP + NS
HA = 4
HF = 8
HD = 64
PAGE = 128
NPAGE = 8
EPS = 1e-6
NEXP = 32
TOPK = 4
SLOTS = 64
MAXPASS = -(-T // SLOTS)
QKV = 3 * HA * P
C_Z, C_BA, C_QF = QKV, QKV + 512, QKV + 512 + 8
C_KF, C_VF = C_QF + 512, C_QF + 1024
C_FF = C_VF + 512
C_GA = C_FF + HF
C_GF = C_GA + D
CHUNKS = [(0, P), (P, P), (2 * P, NP - 2 * P)]
ROWS = [(0, 0, 0, P), (1, 0, P, P), (2, 0, 2 * P, 16), (2, 32, NP, NS)]


class Sems(dict):

    def __init__(self, nc):
        super().__init__()
        self.nc = nc

    def __missing__(self, name):
        self[name] = self.nc.alloc_semaphore(name)
        return self[name]

    def renew(self):
        self.nc.clear_and_free_semaphores(list(self.values()))
        self.nc.all_engine_barrier()
        self.clear()


class Steps:

    def __init__(self, eng, sem, base=0):
        self.eng, self.sem, self.n, self.base = eng, sem, 0, base

    def step(self, ins):
        ins.then_inc(self.sem, 1)
        self.n += 1
        return ins

    def settle(self):
        self.eng.wait_ge(self.sem, self.base + self.n)

    def link(self, ins):
        self.step(ins)
        self.settle()


def spread(ap, axis, n):
    a = ap.unsqueeze(axis)
    return a.to_broadcast([*a.shape[:axis], n, *a.shape[axis + 1:]])


def program(nc, i, o, stop=99):
    with ExitStack() as ctx:
        build(nc, i, o, ctx, stop)


def build(nc, i, o, ctx, stop):
    S = Sems(nc)

    def sb(name, shape, dt=F32, c=ctx):
        return c.enter_context(nc.sbuf_tensor(name, shape, dt))

    bank = [ctx.enter_context(nc.psum_tensor(f"bank{n}", [P, 512], F32)) for n in range(8)]

    def ps(n, parts, *dims):
        size = 1
        for d in dims:
            size *= d
        a = bank[n][0:parts, 0:size]
        if len(dims) == 2:
            a = a.rearrange("p (a b) -> p a b", a=dims[0])
        if len(dims) == 3:
            a = a.rearrange("p (a b c) -> p a b c", a=dims[0], b=dims[1])
        return a

    h_dram = nc.dram_tensor("h_dram", [2 * P + 40, D], F32).ap()
    y_dram = nc.dram_tensor("y_dram", [1 + TOPK * (2 * P + 40), 2, D // 2], F32).ap()

    wg = sb("wg", [P, KT, D])
    wu = sb("wu", [P, KT, D])
    wd = sb("wd", [P, KT, D])
    xr = sb("xr", [P, 3, D])
    pts = sb("pts", [1, NS * NPAGE], I32)
    ident = sb("ident", [P, P])
    ones = sb("ones", [P, P])
    tri = sb("tri", [P, P])
    tris = sb("tris", [P, P])
    epsb = sb("epsb", [P, 1])
    iota64 = sb("iota64", [P, SLOTS])
    iota_i = sb("iota_i", [P, P], I32)
    part_i = sb("part_i", [P, P], I32)
    w4 = sb("w4", [P, 3, TOPK])
    code = sb("code", [P, 3, NEXP])
    dest = sb("dest", [P, 3, NEXP, 2])
    hi64 = sb("hi64", [P, 1])
    cnt_i = sb("cnt_i", [P, 1], I32)
    ring = wg[:, :, :].rearrange("p k (s n) -> p s k n", s=2)
    qB = wu[:, 0:4, :].rearrange("p k (a n) -> p (k a) n", a=2)
    sS = wu[:, 4:8, :].rearrange("p k (a n) -> p (k a) n", n=P)
    kc = wd[:, :, :].rearrange("p (s a) (c n) -> p s (a c) n", s=4, c=2)

    mix = ctx.enter_context(ExitStack())
    co = sb("co", [P, 12, T], c=mix)
    zs = sb("zs", [P, HA, T], c=mix)
    sg = sb("sg", [P, 16, T], c=mix)
    qk = sb("qk", [P, 8, T], c=mix)
    vr = sb("vr", [P, 3, 512], c=mix)
    vD = sb("vD", [NS, 512], c=mix)
    kD = sb("kD", [NS, 512], c=mix)
    qD = sb("qD", [NS, 512], c=mix)
    smz = sb("smz", [P, 4, 16], c=mix)
    sml = sb("sml", [P, 4, 16], c=mix)
    sm = sb("sm", [P, 4, 16], c=mix)
    lfc = sb("lfc", [P, HF, NS, NPAGE], c=mix)
    sc = sb("sc", [P, HF, NS, NPAGE], c=mix)
    hr = sg[:, :, :].rearrange("p a b -> p (a b)")[:, 0:3 * D].rearrange("p (t n) -> p t n", t=3)

    blk1 = ctx.enter_context(ExitStack())
    hT = sb("hT", [P, KT, T], c=blk1)
    xe = sb("xe", [P, 12, 3 + NP], c=blk1)
    xs = sb("xs", [P, 12, NS, 4], c=blk1)
    xsw = sb("xsw", [P, 12, NS, 4], c=blk1)
    cwt = sb("cwt", [P, 12, 28], c=blk1)
    cr = co[0:28, :, :].rearrange("p a b -> p (a b)")[:, 0:QKV]
    cvrows = sb("cvrows", [35, QKV], c=blk1)
    cvp, cvs = cvrows[32:35, :], cvrows[0:NS, :]
    early = sg[:, :, :].rearrange("p a b -> p (a b)")
    sq = early[:, 0:4 * T].rearrange("p (a b) -> p a b", a=4)
    rr = early[:, 4 * T:6 * T].rearrange("p (a b) -> p a b", a=2)
    kro = [early[:, 6 * T:6 * T + 512], early[:, 6 * T + 512:6 * T + 1024], vr[32:48, 2]]
    bd64 = sb("bd64", [P, P], c=blk1)
    wsm = sb("wsm", [P, KT, 16], c=blk1)
    gmix = sb("gmix", [P, KT], c=blk1)
    ss = sb("ss", [P, 4], c=blk1)
    bias16 = sb("bias16", [P, 16], c=blk1)
    ea = sb("ea", [P, 4], c=blk1)
    gq = sb("gq", [P, 2], c=blk1)
    ptc = sb("ptc", [NS * NPAGE, 1], I32, c=blk1)
    lfp = sg[0:NS * NPAGE, :, :].rearrange("p a b -> p (a b)")[:, 3 * D:4 * D]

    w_in = i["w_in"][0].rearrange("(p k) n -> p k n", k=KT)
    cols = [C_QF, C_KF, C_VF, 0, 512, 1024, C_Z, C_GA, C_GA + 512, C_GF, C_GF + 512]
    ck = i["cache_k"][0].rearrange("n t h d -> n t (h d)")
    cv = i["cache_v"][0].rearrange("n t h d -> n t (h d)")

    order = {
        "proj": [f"{x}{n}" for x, m in (("q", 4), ("k", 4), ("v", 3), ("A", 12), ("z", 4), ("g", 16)) for n in range(m)],
        "a": [f"nq{n}" for n in range(4)] + [f"nk{n}" for n in range(4)] + ["qD", "kD", "cvp0", "cvs0"]
             + [f"qB{n}" for n in range(NS)] + ["cvp1", "cvs1"] + [f"krow{n}" for n in range(3)] + ["cvp2", "cvs2"]
             + [f"na{n}" for n in range(8)],
        "v": ["small", "cw", "lf"],
    }
    last_of_chunk = ["q3", "k3", "v2", "A3", "A7", "A11", "z3", "g3", "g7", "g11", "g15"]
    first_bank = {"proj": (0, 4), "a": (4, 2), "v": (6, 2)}

    def bank_of(kind, name):
        b, n = first_bank[kind]
        return b + order[kind].index(name) % n

    def fill_wait(eng, kind, name):
        n = order[kind].index(name) + 1 - first_bank[kind][1]
        if n > 0:
            eng.wait_ge(S[kind + "_evac"], n)

    def full_wait(eng, kind, name):
        eng.wait_ge(S[kind + "_full"], order[kind].index(name) + 1)

    def evac_wait(eng, kind, name):
        eng.wait_ge(S[kind + "_evac"], order[kind].index(name) + 1)

    with nc.Block() as block:

        @block.sync
        def _(sp):
            sp.dma_start(xr[0:NMETA, 0, :], i["meta_tokens"]).then_inc(S["x0_in"], 16)
            sp.dma_start(xr[NMETA:P, 0, :], i["x_prompt"][0, 0:P - NMETA, :]).then_inc(S["x0_in"], 16)
            sp.dma_start(xr[:, 1, :], i["x_prompt"][0, P - NMETA:2 * P - NMETA, :]).then_inc(S["x1_in"], 16)
            sp.wait_ge(S["x2_zeroed"], 1)
            sp.dma_start(xr[0:16, 2, :], i["x_prompt"][0, 2 * P - NMETA:, :]).then_inc(S["x2_in"], 16)
            sp.dma_start(xr[32:32 + NS, 2, :], i["x_sample"].rearrange("b t d -> (b t) d")).then_inc(S["x2_in"], 16)
            sp.dma_start(gmix[:, :], i["g_mix"][0].rearrange("(p k) -> p k", k=KT)).then_inc(S["gmix_in"], 16)

            def weights(n):
                sp.dma_start(ring[:, n % 2], w_in[:, :, cols[n]:cols[n] + 512]).then_inc(S[f"w{n % 2}_in"], 16)

            weights(0)
            sp.dma_start(wsm[:, :, 0:8], w_in[:, :, C_BA:C_BA + 8]).then_inc(S["wsm_in"], 16)
            sp.dma_start(wsm[:, :, 8:16], w_in[:, :, C_FF:C_FF + 8]).then_inc(S["wsm_in"], 16)
            sp.wait_ge(S["bias16_zeroed"], 1)
            sp.dma_start(bias16[:, 4:8], i["dt_bias"].to_broadcast([P, HA])).then_inc(S["bias_in"], 16)
            sp.dma_start(bias16[:, 8:16], i["b_forget"].to_broadcast([P, HF])).then_inc(S["bias_in"], 16)
            sp.dma_start(ea[:, :], i["a_log"].to_broadcast([P, HA])).then_inc(S["alog_in"], 16)
            for half in range(2):
                sp.dma_start(gq[64 * half:64 * half + 64, 0:1], i["qn_g"].rearrange("a d -> d a")).then_inc(S["gq_in"], 16)
                sp.dma_start(gq[64 * half:64 * half + 64, 1:2], i["kn_g"].rearrange("a d -> d a")).then_inc(S["gq_in"], 16)
            sp.dma_start(pts[:, :], i["page_table"].rearrange("(o b) n -> o (b n)", o=1)).then_inc(S["pts_in"], 16)
            sp.dma_start(ptc[:, :], i["page_table"].rearrange("b (n o) -> (b n) o", o=1)).then_inc(S["ptc_in"], 16)
            weights(1)
            sp.dma_start(cr[0:4, :], i["conv_w"][0]).then_inc(S["cr_in"], 16)
            sp.dma_start(cr[4:28, :], i["state_conv"][0].rearrange("b w c -> (b w) c")).then_inc(S["cr_in"], 16)
            sp.dma_start(sS, i["state_delta"][0].rearrange("b h k v -> k (b h) v")).then_inc(S["sS_in"], 16)
            sp.dma_start(o["conv_sample"][0, :, 0:2, :], i["state_conv"][0, :, 1:3, :]).then_inc(S["stored"], 16)
            sp.wait_ge(S["pts_in"], 16)

            def key_pages(b2, s):
                for j in range(4):
                    page = sp.value_load(pts[0:1, bass.ds(b2 * 16 + (s * 4 + j), 1)], min_val=0,
                                         max_val=i["cache_k"].shape[1] - 1)
                    sp.dma_start(kc[:, s, j], ck[bass.ds(page, 1)].rearrange("o t x -> t (o x)")).then_inc(
                        S[f"kslot{s}_in"], 16)

            for s in range(4):
                key_pages(0, s)
            with sp.Fori(1, NS // 2) as b2:
                for s in range(4):
                    sp.wait_ge(S[f"kslot{s}_used"], b2)
                    key_pages(b2, s)
            for t, _, c0, n in ROWS[:3]:
                sp.wait_ge(S["sm_done"], 1)
                sp.dma_start(o["logf_prompt"][0, 0, c0:c0 + n], sm[0:n, t, 8:16]).then_inc(S["stored"], 16)
            sp.dma_start(o["logf_sample"][0, :, 0], sm[0:NS, 3, 8:16]).then_inc(S["stored"], 16)
            evac_wait(sp, "a", "cvs2")
            sp.dma_start(o["conv_prompt"][0, 0], cvp).then_inc(S["stored"], 16)
            sp.dma_start(o["conv_sample"][0, :, 2, :], cvs).then_inc(S["stored"], 16)
            sp.wait_ge(S["stored"], 16 * 7)
            sp.wait_ge(S["rows_stored"], 16 * 8)
            sp.wait_ge(S["sS_in"], 16)

        @block.gpsimd
        def _(pool):
            me = Steps(pool, S["pool1"])
            nc.gpsimd.memset(xr[:, 2, :], 0.0).then_inc(S["x2_zeroed"], 1)
            nc.gpsimd.memset(bias16[:, :], 0.0).then_inc(S["bias16_zeroed"], 1)
            nc.gpsimd.memset(epsb[:, :], EPS).then_inc(S["epsb_set"], 1)
            me.step(nc.gpsimd.memset(ident[:, :], 0.0))
            me.step(nc.gpsimd.memset(tri[:, :], 1.0))
            me.step(nc.gpsimd.memset(tris[:, :], 1.0))
            nc.gpsimd.memset(ones[:, :], 1.0).then_inc(S["consts"], 1)
            me.settle()
            nc.gpsimd.affine_select(out=ident[:, :], in_=ident[:, :], compare_op=ALU.not_equal, fill=1.0, base=0,
                                    pattern=[[-1, P]], channel_multiplier=1).then_inc(S["consts"], 1)
            nc.gpsimd.affine_select(out=tri[:, :], in_=tri[:, :], compare_op=ALU.is_ge, fill=0.0, base=0,
                                    pattern=[[1, P]], channel_multiplier=-1).then_inc(S["consts"], 1)
            nc.gpsimd.affine_select(out=tris[:, :], in_=tris[:, :], compare_op=ALU.is_gt, fill=0.0, base=0,
                                    pattern=[[1, P]], channel_multiplier=-1).then_inc(S["consts"], 1)
            nc.gpsimd.memset(xe[:, :, 0:3], 0.0).then_inc(S["consts"], 1)
            nc.gpsimd.memset(smz[:, :, :], 0.0).then_inc(S["smz_zeroed"], 1)
            nc.gpsimd.iota(iota_i[:, :], [[1, P]], 0, 0).then_inc(S["iotas"], 1)
            nc.gpsimd.iota(part_i[:, :], [[0, P]], 0, 1).then_inc(S["iotas"], 1)
            pool.wait_ge(S["ptc_in"], 16)
            nc.gpsimd.indirect_dma_start(
                out=lfp, out_offset=None, in_=i["cache_logf"][0].rearrange("n t h -> n (t h)"),
                in_offset=bass.IndirectOffsetOnAxis(ap=ptc[:, 0:1], axis=0)).then_inc(S["lfp_in"], 16)
            for n in range(2 * NS):
                if n % 2 == 0:
                    evac_wait(pool, "a", f"qB{n // 2}")
                pool.wait_ge(S[f"kslot{n % 4}_in"], (n // 4 + 1) * 64)
                q = spread(qB[:, n // 2], 1, 4)
                nc.gpsimd.tensor_tensor(kc[:, n % 4], kc[:, n % 4], q, ALU.mult).then_inc(S["kprod"], 1)

        @block.scalar
        def _(act):
            me = Steps(act, S["act1"])
            nc.scalar.preload_act_table_set("natural_log_exp_and_others")
            act.wait_ge(S["epsb_set"], 1)
            for t in range(3):
                act.wait_ge(S[f"x{t}_in"], 16 if t == 1 else 32)
                n = P if t < 2 else 40
                me.link(nc.scalar.activation(hr[0:n, t], xr[0:n, t], ACT.Square, accum_out=ss[0:n, t:t + 1]))
                me.link(nc.scalar.activation(ss[0:n, t:t + 1], ss[0:n, t:t + 1], ACT.Ln, scale=1.0 / D, bias=epsb[0:n, :]))
                nc.scalar.activation(ss[0:n, t:t + 1], ss[0:n, t:t + 1], ACT.Exp, scale=-0.5).then_inc(S["rstd_x"], 1)
            act.wait_ge(S["alog_in"], 16)
            nc.scalar.activation(ea[:, :], ea[:, :], ACT.Exp).then_inc(S["ea_done"], 1)
            act.wait_ge(S["sm_abs"], 1)
            me.link(nc.scalar.activation(sml[:, :, :], sml[:, :, :], ACT.Exp))
            nc.scalar.activation(sml[:, :, :], sml[:, :, :], ACT.Ln, bias=1.0).then_inc(S["sm_ln"], 1)
            act.wait_ge(S["sm_logs"], 1)
            nc.scalar.activation(sm[:, :, 0:4], sm[:, :, 0:4], ACT.Exp).then_inc(S["sm_done"], 1)

            def proj(name, put):
                full_wait(act, "proj", name)
                put(bank_of("proj", name)).then_inc(S["proj_evac"], 1)

            def misc(name, put):
                full_wait(act, "a", name)
                put(bank_of("a", name)).then_inc(S["a_evac"], 1)

            def copy(dst, n, m):
                return lambda b: nc.scalar.activation(dst, ps(b, n, m), ACT.Copy)

            def norm(name, scale, r):
                def put(b):
                    me.link(nc.scalar.activation(rr[:, r % 2], ps(b, P, T), ACT.Ln, scale=scale, bias=epsb[:, :]))
                    return nc.scalar.activation(rr[:, r % 2], rr[:, r % 2], ACT.Exp, scale=-0.5)
                if r >= 2:
                    act.wait_ge(S["normed"], r - 1)
                misc(name, put)

            def weights(n):
                act.dma_start(ring[:, n % 2], w_in[:, :, cols[n]:cols[n] + 512]).then_inc(S[f"w{n % 2}_in"], 16)

            def store(dst, src, kind, name):
                evac_wait(act, kind, name)
                act.dma_start(dst.rearrange("t h d -> t (h d)"), src).then_inc(S["rows_stored"], 16)

            for c in range(4):
                proj(f"q{c}", copy(qk[:, c], P, T))
            weights(2)
            for c in range(4):
                proj(f"k{c}", copy(qk[:, 4 + c], P, T))
            weights(3)
            for c in range(4):
                norm(f"nq{c}", 1.0 / HD, c)
            proj("v0", copy(vr[:, 0], P, 512))
            proj("v1", copy(vr[:, 1], P, 512))

            def put_v2(b):
                nc.scalar.activation(vD[:, :], bank[b][32:32 + NS, :], ACT.Copy)
                return nc.scalar.activation(vr[0:16, 2], ps(b, 16, 512), ACT.Copy)
            proj("v2", put_v2)
            weights(4)
            for t, _, c0, n in ROWS[:3]:
                store(o["v_prompt"][0, 0, c0:c0 + n], vr[0:n, t], "proj", f"v{t}")
            store(o["v_sample"][0, :, 0], vD[:, :], "proj", "v2")

            def before(tile):
                if tile < 2:
                    for c in (2 * tile, 2 * tile + 1):
                        norm(f"nk{c}", 1.0 / HD, 4 + c)
                elif tile == 3:
                    misc("qD", copy(qD[:, :], NS, 512))
                    misc("kD", copy(kD[:, :], NS, 512))
                elif 4 <= tile < 8:
                    for b in (2 * tile - 8, 2 * tile - 7):
                        misc(f"qB{b}", copy(qB[:, b], P, 512))
                elif 8 <= tile < 11:
                    t = tile - 8
                    _, _, c0, n = ROWS[t]
                    misc(f"krow{t}", copy(kro[t], n, 512))
                    store(o["k_prompt"][0, 0, c0:c0 + n], kro[t], "a", f"krow{t}")
                elif tile == 11:
                    store(o["k_sample"][0, :, 0], kD[:, :], "a", "kD")

            for part in range(3):
                for c in range(4):
                    before(4 * part + c)
                    def put(b):
                        nc.scalar.activation(xs[:, 4 * part + c, :, 3], bank[b][:, NP:T], ACT.Copy)
                        return nc.scalar.activation(xe[:, 4 * part + c, 3:3 + NP], bank[b][:, 0:NP], ACT.Copy)
                    proj(f"A{4 * part + c}", put)
                weights(5 + part)
                misc(f"cvp{part}", copy(cvp[:, 512 * part:512 * part + 512], 3, 512))
                misc(f"cvs{part}", copy(cvs[:, 512 * part:512 * part + 512], NS, 512))
            for part in range(3):
                act.wait_ge(S["conv_done"], part + 1)
                q = co[:, 4 * part:4 * part + 4]
                nc.scalar.activation(q, q, ACT.Silu).then_inc(S["silu_done"], 1)
            for c in range(4):
                proj(f"z{c}", lambda b: nc.scalar.activation(zs[:, c], ps(b, P, T), ACT.Silu))
            weights(8)
            nc.scalar.preload_act_table_set("natural_log_exp_and_others")
            for c in range(8):
                norm(f"na{c}", 1.0, 8 + c)
            act.wait_ge(S["rows_stored"], 16 * 8)
            act.wait_ge(S["normed"], 16)
            for c in range(16):
                if c in (4, 8):
                    weights(8 + c // 4)
                proj(f"g{c}", lambda b: nc.scalar.activation(sg[:, c], ps(b, P, T), ACT.Sigmoid))

        @block.tensor
        def _(pe):
            mm = nc.tensor.matmul

            def done(kind, last):
                last.then_inc(S[kind + "_full"], 1)

            pe.wait_ge(S["consts"], 4)
            for t in range(3):
                pe.wait_ge(S["h_rows"], t + 1)
                n = P if t < 2 else 40
                for k in range(KT):
                    b = 2 * t + k // 4 if t < 2 else 4
                    dst = bank[b][:, (k % 4) * P:(k % 4) * P + P] if t < 2 else bank[b][:, 64 * k:64 * k + n]
                    last = nc.tensor.transpose(dst, hr[0:n, t].rearrange("p (c k) -> p k c", k=KT)[:, k], ident[0:n, 0:n])
                    if k % 4 == 3 and t < 2 or k == 7:
                        last.then_inc(S["xT_full"], 1)
            pe.wait_ge(S["hT_done"], 5)
            pe.wait_ge(S["wsm_in"], 32)
            b = bank_of("v", "small")
            for t, (_, _, c0, n) in enumerate(ROWS):
                for k in range(KT):
                    last = mm(bank[b][0:n, 16 * t:16 * t + 16], hT[:, k, c0:c0 + n], wsm[:, k], start=k == 0, stop=k == 7)
            done("v", last)
            pe.wait_ge(S["cr_in"], 32)
            b = bank_of("v", "cw")
            for c in range(12):
                last = nc.tensor.transpose(bank[b][:, 28 * c:28 * c + 28], cr[:, P * c:P * c + P], ident[0:28, 0:28])
            done("v", last)
            chunk = [0]

            def chunk_in():
                n = chunk[0]
                chunk[0] += 1
                pe.wait_ge(S[f"w{n % 2}_in"], 16 * (n // 2 + 1))
                return ring[:, n % 2]

            def proj_cols(names, between=lambda c: None):
                w = chunk_in()
                for c, name in enumerate(names):
                    between(c)
                    fill_wait(pe, "proj", name)
                    b = bank_of("proj", name)
                    for k in range(KT):
                        last = mm(ps(b, P, T), w[:, k, P * c:P * c + P], hT[:, k], start=k == 0, stop=k == 7)
                    done("proj", last)

            def sums(name, weights, src):
                fill_wait(pe, "a", name)
                done("a", mm(ps(bank_of("a", name), P, T), weights, src, start=True, stop=True))

            proj_cols([f"q{c}" for c in range(4)])
            proj_cols([f"k{c}" for c in range(4)])
            pe.wait_ge(S["bd64_set"], 2)
            pe.wait_ge(S["sq_done"], 1)
            for c in range(4):
                sums(f"nq{c}", bd64[:, :], sq[:, c])
            w = chunk_in()
            for t in range(2):
                fill_wait(pe, "proj", f"v{t}")
                for k in range(KT):
                    last = mm(ps(bank_of("proj", f"v{t}"), P, 512), hT[:, k, P * t:P * t + P], w[:, k], start=k == 0, stop=k == 7)
                done("proj", last)
            fill_wait(pe, "proj", "v2")
            b = bank_of("proj", "v2")
            for k in range(KT):
                for _, p0, c0, n in ROWS[2:]:
                    last = mm(bank[b][p0:p0 + n, :], hT[:, k, c0:c0 + n], w[:, k], start=k == 0, stop=k == 7)
            done("proj", last)
            def rows_of(name, src, c0, n):
                fill_wait(pe, "a", name)
                b = bank_of("a", name)
                for c in range(4):
                    last = nc.tensor.transpose(bank[b][0:n, P * c:P * c + P], src(c, c0, n), ident[:, :])
                done("a", last)


            def before(tile):
                if tile < 2:
                    pe.wait_ge(S["sq_done"], 2)
                    for c in (2 * tile, 2 * tile + 1):
                        sums(f"nk{c}", bd64[:, :], sq[:, c])
                elif tile == 3:
                    pe.wait_ge(S["normed"], 8)
                    rows_of("qD", lambda c, c0, n: qk[:, c, c0:c0 + n], NP, NS)
                    rows_of("kD", lambda c, c0, n: qk[:, 4 + c, c0:c0 + n], NP, NS)
                elif 4 <= tile < 8:
                    evac_wait(pe, "a", "qD")
                    for b in (2 * tile - 8, 2 * tile - 7):
                        fill_wait(pe, "a", f"qB{b}")
                        done("a", mm(ps(bank_of("a", f"qB{b}"), P, 512), ident[0:NS, b:b + 1].to_broadcast([NS, P]), qD[:, :],
                                     start=True, stop=True))
                elif 8 <= tile < 11:
                    t = tile - 8
                    rows_of(f"krow{t}", lambda c, c0, n: qk[:, 4 + c, c0:c0 + n], ROWS[t][2], ROWS[t][3])
                elif tile == 11:
                    pe.wait_ge(S["lfp_in"], 16)
                    fill_wait(pe, "v", "lf")
                    for h in range(HF):
                        last = nc.tensor.transpose(bank[bank_of("v", "lf")][:, 64 * h:64 * h + 64],
                                                   lfp.rearrange("p (t h) -> p h t", h=HF)[:, h], ident[0:64, 0:64])
                    done("v", last)

            for part in range(3):
                proj_cols([f"A{4 * part + c}" for c in range(4)], lambda c: before(4 * part + c))
                evac_wait(pe, "proj", f"A{4 * part + 3}")
                rows_of(f"cvp{part}", lambda c, c0, n: xe[:, 4 * part + c, NP:NP + 3], 0, 3)
                rows_of(f"cvs{part}", lambda c, c0, n: xs[:, 4 * part + c, :, 3], 0, NS)
            proj_cols([f"z{c}" for c in range(4)])

            def sums_ahead(g):
                for c in (2 * g, 2 * g + 1):
                    pe.wait_ge(S["sq_done"], 3 + c // 4)
                    sums(f"na{c}", ones[:, :], sq[:, c % 4])

            proj_cols([f"g{c}" for c in range(4)], sums_ahead)
            for g in range(1, 4):
                proj_cols([f"g{4 * g + c}" for c in range(4)])

        @block.vector
        def _(dve):
            me = Steps(dve, S["dve1"])
            tt, ts, stt = nc.vector.tensor_tensor, nc.vector.tensor_scalar, nc.vector.scalar_tensor_tensor
            me.link(nc.vector.memset(bd64[:, :], 0.0))
            for half in range(2):
                q = slice(64 * half, 64 * half + 64)
                nc.vector.memset(bd64[q, q], 1.0).then_inc(S["bd64_set"], 1)
            for t in range(3):
                n = P if t < 2 else 40
                dve.wait_ge(S["rstd_x"], t + 1)
                ts(hr[0:n, t], xr[0:n, t], ss[0:n, t:t + 1], None, ALU.mult).then_inc(S["h_rows"], 1)
            dve.wait_ge(S["gmix_in"], 16)
            for q in range(4):
                dve.wait_ge(S["xT_full"], q + 1)
                k0, c0 = 4 * (q % 2), P * (q // 2)
                tt(hT[:, k0:k0 + 4, c0:c0 + P], ps(q, P, 4, P), spread(gmix[:, k0:k0 + 4], 2, P), ALU.mult).then_inc(S["hT_done"], 1)
            dve.wait_ge(S["xT_full"], 5)
            src = ps(4, P, KT, 64)
            tt(hT[:, :, 256:272], src[:, :, 0:16], spread(gmix[:, :], 2, 16), ALU.mult)
            tt(hT[:, :, 272:280], src[:, :, 32:40], spread(gmix[:, :], 2, NS), ALU.mult).then_inc(S["hT_done"], 1)

            full_wait(dve, "v", "small")
            dve.wait_ge(S["bias_in"], 32)
            dve.wait_ge(S["smz_zeroed"], 1)
            b = bank_of("v", "small")
            for t, (_, _, _, n) in enumerate(ROWS):
                ins = tt(smz[0:n, t], bank[b][0:n, 16 * t:16 * t + 16], bias16[0:n, :], ALU.add)
            ins.then_inc(S["v_evac"], 1)
            evac_wait(dve, "v", "small")
            stt(sml[:, :, :], smz[:, :, :], -1.0, smz[:, :, :], ALU.mult, ALU.min).then_inc(S["sm_abs"], 1)
            full_wait(dve, "v", "cw")
            src = ps(bank_of("v", "cw"), P, 12, 28)
            nc.vector.tensor_copy(cwt[:, :, :], src)
            for c in range(12):
                ins = nc.vector.tensor_copy(xs[:, c, :, 0:3], src[:, c, 4:28].rearrange("p (b w) -> p b w", w=3))
            ins.then_inc(S["v_evac"], 1)
            dve.wait_ge(S["sm_ln"], 1)
            dve.wait_ge(S["ea_done"], 1)
            stt(sm[:, :, 0:4], smz[:, :, 0:4], 0.0, sml[:, :, 0:4], ALU.min, ALU.subtract)
            stt(sm[:, :, 8:16], smz[:, :, 8:16], 0.0, sml[:, :, 8:16], ALU.min, ALU.subtract)
            me.link(stt(sm[:, :, 4:8], smz[:, :, 4:8], 0.0, sml[:, :, 4:8], ALU.max, ALU.add))
            stt(sm[:, :, 4:8], sm[:, :, 4:8], -1.0, spread(ea[:, :], 1, 4), ALU.mult, ALU.mult).then_inc(S["sm_logs"], 1)

            def squares(src):
                tt(sq[:, :, :], src, src, ALU.mult).then_inc(S["sq_done"], 1)

            def normalize(dst, name, gain, n):
                evac_wait(dve, "a", name)
                stt(dst, rr[:, n % 2], gain, dst, ALU.mult, ALU.mult).then_inc(S["normed"], 1)

            dve.wait_ge(S["gq_in"], 64)
            me.link(ts(gq[:, 0:1], gq[:, 0:1], HD ** -0.5, None, ALU.mult))
            evac_wait(dve, "proj", "q3")
            squares(qk[:, 0:4])
            for c in range(4):
                normalize(qk[:, c], f"nq{c}", gq[:, 0:1], c)
            evac_wait(dve, "proj", "k3")
            squares(qk[:, 4:8])
            for c in range(4):
                normalize(qk[:, 4 + c], f"nk{c}", gq[:, 1:2], 4 + c)

            def key_sums(n):
                dve.wait_ge(S["kprod"], n + 1)
                nc.vector.tensor_reduce(sc[:, :, n // 2, 4 * (n % 2):4 * (n % 2) + 4].rearrange("p h n -> p n h"),
                                        kc[:, n % 4].rearrange("p n (h d) -> p n h d", h=HF), AX.X, ALU.add
                                        ).then_inc(S[f"kslot{n % 4}_used"], 1)

            dve.wait_ge(S["consts"], 5)
            for part in range(3):
                evac_wait(dve, "proj", f"A{4 * part + 3}")
                for w in range(4):
                    for c in range(4 * part, 4 * part + 4):
                        if w == 0:
                            ins = ts(co[:, c, 0:NP], xe[:, c, 0:NP], cwt[:, c, 0:1], None, ALU.mult)
                        else:
                            ins = stt(co[:, c, 0:NP], xe[:, c, w:w + NP], cwt[:, c, w:w + 1], co[:, c, 0:NP], ALU.mult, ALU.add)
                    me.link(ins)
                q = slice(4 * part, 4 * part + 4)
                me.link(tt(xsw[:, q], xs[:, q], spread(cwt[:, q, 0:4], 2, NS), ALU.mult))
                nc.vector.tensor_reduce(co[:, q, NP:T], xsw[:, q], AX.X, ALU.add).then_inc(S["conv_done"], 1)
                for n in range((0, 0, 3)[part], (0, 3, 6)[part]):
                    key_sums(n)
            full_wait(dve, "v", "lf")
            nc.vector.tensor_copy(lfc[:, :, :, :].rearrange("p h b n -> p (h b n)"), ps(bank_of("v", "lf"), P, 512)).then_inc(S["v_evac"], 1)
            dve.wait_ge(S["silu_done"], 1)
            squares(co[:, 0:4])
            for c in range(4):
                normalize(co[:, c], f"na{c}", P ** -0.5, 8 + c)
            dve.wait_ge(S["silu_done"], 2)
            squares(co[:, 4:8])
            for c in range(4):
                normalize(co[:, 4 + c], f"na{4 + c}", 1.0, 12 + c)
            for n in range(6, 2 * NS):
                key_sums(n)

    blk1.close()
    if stop < 2:
        return
    blk2 = ctx.enter_context(ExitStack())
    pa = wg[:, 4:8, :]
    scratch = wg[:, 0:4, :].rearrange("p k n -> p (k n)")
    used = [0]

    def cut(n, parts=P):
        a = scratch[0:parts, used[0]:used[0] + n]
        used[0] += n
        assert used[0] <= 4 * D
        return a

    four = "p (a b) -> p a b"
    pr = [cut(656), cut(656)]
    pT = [cut(432), cut(432)]
    EGB = cut(512).rearrange(four, a=4)
    raw = cut(512).rearrange(four, a=4)
    dec = cut(512).rearrange(four, a=4)
    xorf = cut(128)
    lows = cut(128)
    qBf = wu[:, 0:4, :].rearrange("p k n -> p (k n)")
    Am = [qBf[:, 512 * c:512 * c + 512].rearrange(four, a=4) for c in range(2)]
    Em = [qBf[:, 1024 + 512 * c:1536 + 512 * c].rearrange(four, a=4) for c in range(2)]
    Mm = [qBf[:, 2048 + 512 * c:2560 + 512 * c].rearrange(four, a=4) for c in range(2)]
    Kr = [qBf[:, 3072 + 512 * c:3584 + 512 * c].rearrange(four, a=4) for c in range(2)]
    U = [sb(f"U{c}", [P, 4, P], c=blk2) for c in range(2)]
    Tm = [sb(f"Tm{c}", [P, 4, P], c=blk2) for c in range(2)]
    PT = [sb(f"PT{c}", [P, 4, P], c=blk2) for c in range(2)]
    Vb = [sb(f"Vb{c}", [P, 4, P], c=blk2) for c in range(2)]
    small = sb("small", [16, 6, 4, 16], c=blk2)
    Am.append(small[:, 0]); Em.append(small[:, 1]); Mm.append(small[:, 2]); U.append(small[:, 3]); PT.append(small[:, 4]); Tm.append(small[:, 5])
    kv2 = sb("kv2", [16, 2, 4, P], c=blk2)
    Kr.append(kv2[:, 0]); Vb.append(kv2[:, 1])
    Rm = sb("Rm", [P, 4, P], c=blk2)
    dl = sb("dl", [P, 4, P], c=blk2)
    St = sb("St", [P, 4, P], c=blk2)
    Gc = sb("Gc", [P, 3, 4], c=blk2)
    kd = sb("kd", [P, 3, 4], c=blk2)
    nbe = sb("nbe", [P, 3, 4], c=blk2)
    gend = sb("gend", [P, 3, 4], c=blk2)
    nmask = sb("nmask", [P, P], c=blk2)
    ncT = sb("ncT", [HF, NP], c=blk2)
    mx = sb("mx", [P, 2, 3], c=blk2)
    ls = sb("ls", [P, 2, 3], c=blk2)
    rfx = sb("rfx", [P, HF, NS, NPAGE], c=blk2)
    ex8 = sb("ex8", [NS, 24, NS], c=blk2)
    m64 = qBf[:, 0:512].rearrange("p (a b) -> p a b", a=8)
    bge = sb("bge", [P, 8, NS], c=blk2)
    vT = sb("vT", [P, 4, NS], c=blk2)
    s32 = sb("s32", [P, 6, 4, NS], c=blk2)
    Dx = qBf[0:NS, 1024:2048].rearrange("p (a b) -> p a b", a=NS)
    dD = qBf[0:NS, 2048:3072].rearrange("p (a b) -> p a b", a=2)
    egr = sb("egr", [NS, 4], c=blk2)
    nga = sb("nga", [P, 1], c=blk2)
    sq2 = EGB.rearrange("p a b -> p (a b)")[:, 0:T]
    rr2 = raw.rearrange("p a b -> p (a b)")[:, 0:T]
    pn, mall, lrec, snb, m1 = (m64[:, n] for n in range(5))
    mcol = m64[0:64, 5, 0:1]
    mdiag = m64[0:64, 6, 0:64]
    lsum = m64[:, 7]
    prod8 = Rm[0:NS].rearrange("p a b -> p (a b)")

    def levels(c):
        return 7 if c < 2 else 4

    def tbank(c, n):
        if c == 2:
            return bank[7][0:n, 64:64 + 4 * n].rearrange("p (a b) -> p a b", a=4)
        return ps(6 if c == 0 else 2, n, 4, n)

    stage = [dec.rearrange("p a b -> p (a b)"), pr[1][:, 0:512]]
    stage4 = [a.rearrange("p (n h b) -> p n h b", n=NPAGE, h=HF) for a in stage]
    vsum = pr[0][:, 0:512]
    ident2 = pT[0][:, 0:64]

    with nc.Block() as block:

        def score_banks(h):
            b = 2 * ((h + 2) % 3)
            return b, b + 1

        def fcopy(act, h):
            act.wait_ge(S["fT_full"], h + 1)
            t_, bk = pT[h % 2], bank[6]
            nc.scalar.activation(t_[:, 0:416], bk[:, 0:416], ACT.Copy)
            nc.scalar.activation(t_[0:16, 416:432], bk[0:16, 416:432], ACT.Copy).then_inc(S["fcopy"], 1)

        def value_pages(eng, b2, s):
            for j in range(4):
                page = eng.value_load(pts[0:1, bass.ds(b2 * 16 + (s * 4 + j), 1)], min_val=0,
                                      max_val=i["cache_v"].shape[1] - 1)
                eng.dma_start(kc[:, s, j], cv[bass.ds(page, 1)].rearrange("o t x -> t (o x)")).then_inc(
                    S[f"vslot{s}_in"], 16)

        @block.sync
        def _(sp):
            sp.dma_start(nga[:, :], i["norm_a"].rearrange("a d -> d a")).then_inc(S["nga_in"], 16)
            sp.dma_start(pa, i["p_a"][0].rearrange("(k p) n -> p k n", p=P)).then_inc(S["pa_in"], 16)
            for s in (0, 1):
                value_pages(sp, 0, s)
            with sp.Fori(1, NS // 2) as b2:
                for s in (0, 1):
                    sp.wait_ge(S[f"vslot{s}_used"], b2)
                    value_pages(sp, b2, s)
            sp.wait_ge(S["scan_S"], 3)
            sp.dma_start(o["delta_prompt"][0, 0].rearrange("h k v -> k h v"), St[:, :, :]).then_inc(S["stored2"], 16)
            sp.wait_ge(S["sS_done"], 4)
            sp.wait_ge(S["vslot3_in"], NS // 2 * 64)
            sp.dma_start(o["delta_sample"][0].rearrange("b h k v -> k (b h) v"), sS).then_inc(S["stored2"], 16)
            sp.wait_ge(S["stored2"], 32)
            sp.wait_ge(S["pa_in"], 16)

        @block.gpsimd
        def _(pool):
            for c in range(3):
                n = CHUNKS[c][1]
                nc.gpsimd.tensor_copy(U[c][0:n], spread(ident[0:n, 0:n], 1, 4)).then_inc(S["U_set"], 1)
                nc.gpsimd.tensor_copy(Tm[c][0:n], spread(ident[0:n, 0:n], 1, 4)).then_inc(S["U_set"], 1)
            for c in range(3):
                n = CHUNKS[c][1]
                pool.wait_ge(S["decT"], c + 1)
                pool.wait_ge(S["rows_evac"], c + 1)
                nc.gpsimd.tensor_tensor(Kr[c][0:n], Kr[c][0:n], spread(kd[0:n, c], 2, P), ALU.mult).then_inc(S["Kr_Vb"], 1)
                nc.gpsimd.tensor_tensor(Vb[c][0:n], Vb[c][0:n], spread(sm[0:n, c, 0:4], 2, P), ALU.mult).then_inc(S["Kr_Vb"], 1)
            for lv in range(max(levels(c) for c in range(3))):
                for c in range(3):
                    n = CHUNKS[c][1]
                    if lv + 1 < levels(c):
                        pool.wait_ge(S[f"E{c}"], lv + 1)
                        nc.gpsimd.tensor_tensor(Am[c][0:n], Am[c][0:n], Em[c][0:n], ALU.subtract).then_inc(S[f"A{c}"], 1)
            for s in (2, 3):
                value_pages(pool, 0, s)
            with pool.Fori(1, NS // 2) as b2:
                for s in (2, 3):
                    pool.wait_ge(S[f"vslot{s}_used"], b2)
                    pool.sem_inc(S[f"vslot{s}_asked"], 1)
                    value_pages(pool, b2, s)

        @block.scalar
        def _(act):
            me = Steps(act, S["act2"])
            Exp, Copy = ACT.Exp, ACT.Copy
            nc.scalar.preload_act_table_set("natural_log_exp_and_others")
            nc.scalar.activation(egr[:, :], sm[0:NS, 3, 4:8], Exp).then_inc(S["egr"], 1)

            def rows(c):
                n = CHUNKS[c][1]
                act.wait_ge(S["rows_full"], c + 1)
                b = (6, 4, 6)[c]
                nc.scalar.activation(Kr[c][0:n], ps(b, n, 4, P), Copy)
                nc.scalar.activation(Vb[c][0:n], ps(b + 1, n, 4, P), Copy).then_inc(S["rows_evac"], 1)

            for c, (c0, n) in enumerate(CHUNKS):
                b0 = 4 * (c % 2)
                act.wait_ge(S["prep_full"], c + 1)
                if c:
                    act.wait_ge(S["qg_done"], c)
                me.link(nc.scalar.activation(EGB[:, :, 0:n], ps(b0 + 2, P, 4, n), Exp))
                nc.scalar.activation(gend[:, c], EGB[:, :, n - 1], Copy).then_inc(S["EGB"], 1)
                if c == 0:
                    rows(0)
                act.wait_ge(S["raw_pos"], c + 1)
                nc.scalar.activation(dec[0:n, :, 0:n], dec[0:n, :, 0:n], Exp, scale=-1.0).then_inc(S["decA"], 1)
                act.wait_ge(S["raw_neg"], c + 1)
                nc.scalar.activation(raw[0:n, :, 0:n], raw[0:n, :, 0:n], Exp)
                act.wait_ge(S["kd_arg"], c + 1)
                nc.scalar.activation(nbe[0:n, c], Gc[0:n, c], Exp)
                nc.scalar.activation(kd[0:n, c], kd[0:n, c], Exp).then_inc(S["decT"], 1)
                if c == 0:
                    rows(1)
                    rows(2)
            for lv in range(7):
                for c, (c0, n) in enumerate(CHUNKS):
                    if lv < levels(c):
                        act.wait_ge(S[f"M{c}"], lv + 1)
                        nc.scalar.activation(Mm[c][0:n], ps([0, 4, 3][c], n, 4, n), Copy).then_inc(S[f"Mc{c}"], 1)
            for c, (c0, n) in enumerate(CHUNKS):
                act.wait_ge(S["dl_full"], c + 1)
                nc.scalar.activation(dl[0:n], ps(1, n, 4, P), Copy).then_inc(S["dl"], 1)
                act.wait_ge(S["oT_full"], c + 1)
                nc.scalar.activation(co[:, 8:12, c0:c0 + n], ps(2, P, 4, n), Copy).then_inc(S["oT"], 1)
            for h in range(HF + 2):
                if h >= 2:
                    fcopy(act, h - 2)
                if h >= HF:
                    continue
                act.wait_ge(S["fmax"], h + 1)
                bx, by = score_banks(h)
                p_, m_, l_ = pr[h % 2], mx[:, h % 2], ls[:, h % 2]
                nc.scalar.activation(p_[:, 0:128], bank[bx][:, 0:128], Exp, bias=m_[:, 0:1], accum_out=l_[:, 0:1])
                nc.scalar.activation(p_[:, 128:384], bank[bx][:, 128:384], Exp, bias=m_[:, 1:2], accum_out=l_[:, 1:2])
                nc.scalar.activation(p_[0:16, 384:656], bank[by][0:16, 0:272], Exp, bias=m_[0:16, 2:3],
                                     accum_out=l_[0:16, 2:3]).then_inc(S["fexp"], 1)
            act.wait_ge(S["s_arg"], 1)
            nc.scalar.activation(sc[:, :, :, :], sc[:, :, :, :], Exp)
            nc.scalar.activation(pn, pn, Exp).then_inc(S["s_exp"], 1)
            for c in range(4):
                if c == 3:
                    act.wait_ge(S["vslot3_used"], NS // 2)
                    nc.scalar.activation(vsum, ps(6, P, 512), Copy).then_inc(S["vsum"], 1)
                act.wait_ge(S["osum"], c + 1)
                if c:
                    act.wait_ge(S["oa_done"], c)
                me.link(nc.scalar.activation(rr2, ps(4 + c % 2, P, T), ACT.Ln, scale=1.0 / P, bias=epsb[:, :]))
                nc.scalar.activation(rr2, rr2, Exp, scale=-0.5).then_inc(S["orr"], 1)

        @block.tensor
        def _(pe):
            mm, tr = nc.tensor.matmul, nc.tensor.transpose

            def rows(c):
                c0, n = CHUNKS[c]
                b = (6, 4, 6)[c]
                if c == 2:
                    pe.wait_ge(S["rows_evac"], 1)
                for h in range(HA):
                    tr(bank[b][0:n, P * h:P * h + P], co[:, 4 + h, c0:c0 + n], ident[:, :])
                    last = tr(bank[b + 1][0:n, P * h:P * h + P], co[:, 8 + h, c0:c0 + n], ident[:, :])
                last.then_inc(S["rows_full"], 1)

            for c, (c0, n) in enumerate(CHUNKS):
                b0 = 4 * (c % 2)
                if c == 1:
                    for r in range(3):
                        rows(r)
                    pe.wait_ge(S["rows_evac"], 3)
                if c == 2:
                    pe.wait_ge(S["prep_used"], 1)
                g = sm[0:n, c, 4:8]
                for h in range(HA):
                    k_, q_ = co[:, 4 + h, c0:c0 + n], co[:, h, c0:c0 + n]
                    mm(ps(b0, n, 4, n)[:, h], k_, k_, start=True, stop=True)
                    mm(ps(b0 + 1, n, 4, n)[:, h], k_, q_, start=True, stop=True)
                    mm(ps(b0 + 2, P, 4, n)[:, h], g[:, h:h + 1].to_broadcast([n, P]), tri[0:n, 0:n], start=True, stop=True)
                mm(ps(b0 + 3, n, 4), tri[0:n, 0:n], g, start=True, stop=True).then_inc(S["prep_full"], 1)
            lf = [sm[0:CHUNKS[t][1], t, 8:16] for t in range(3)]
            b7 = bank[7][0:HF, P:P + NP]
            pe.wait_ge(S["prep_used"], 2)
            for s, (s0, n) in enumerate(CHUNKS):
                for t in range(s + 1):
                    m = CHUNKS[t][1]
                    last = mm(b7[:, s0:s0 + n], lf[t], (tri if t == s else ones)[0:m, 0:n], start=t == 0, stop=t == s)
            last.then_inc(S["cT_full"], 1)
            pe.wait_ge(S["prep_used"], 3)
            pe.wait_ge(S["U_set"], 6)
            for lv in range(7):
                for c, (c0, n) in enumerate(CHUNKS):
                    if lv < levels(c):
                        pe.wait_ge(S[f"E{c}"], lv + 1)
                        if lv:
                            pe.wait_ge(S[f"U{c}"], lv)
                        for h in range(HA):
                            last = mm(ps([0, 4, 3][c], n, 4, n)[:, h], Em[c][0:n, h, 0:n], U[c][0:n, h, 0:n], start=True, stop=True)
                        last.then_inc(S[f"M{c}"], 1)
                if lv == 0:
                    pe.wait_ge(S["ncT"], 1)
                for c, (c0, n) in enumerate(CHUNKS):
                    if lv < levels(c):
                        pe.wait_ge(S[f"Mc{c}"], lv + 1)
                        for h in range(HA):
                            last = mm(ps([1, 5, 7][c], n, 4, n)[:, h], Tm[c][0:n, h, 0:n], Mm[c][0:n, h, 0:n], start=True, stop=True)
                        if lv + 1 < levels(c):
                            for h in range(HA):
                                last = mm(tbank(c, n)[:, h], Mm[c][0:n, h, 0:n], Tm[c][0:n, h, 0:n], start=True, stop=True)
                        last.then_inc(S[f"UU{c}"], 1)

            def scores(h, qt):
                hp, j = 64 * (h % 2), h // 2
                bx, by = score_banks(h)
                q0, nq = CHUNKS[qt]
                nk = q0 + nq
                dst = bank[by][0:nq, 0:nk] if qt == 2 else bank[bx][:, (0, 128)[qt]:(0, 128)[qt] + nk]
                mm(dst, qk[hp:hp + 64, j, q0:q0 + nq], qk[hp:hp + 64, 4 + j, 0:nk], start=True, stop=False)
                mm(dst, ident[0:HF, h:h + 1].to_broadcast([HF, nq]), ncT[:, 0:nk], start=False, stop=False)
                last = mm(dst[:, q0:nk], ident[0:nq, 0:nq], nmask[0:nq, 0:nq], start=False, stop=True)
                if qt == 2:
                    last.then_inc(S["fs_full"], 1)

            for c in range(3):
                pe.wait_ge(S[f"U{c}"], levels(c))
            for c, (c0, n) in enumerate(CHUNKS):
                if c:
                    pe.wait_ge(S["scan_S"], c)
                    for h in range(HA):
                        last = mm(ps(0, n, 4, P)[:, h], co[:, 4 + h, c0:c0 + n], St[:, h], start=True, stop=True)
                    last.then_inc(S["kS_full"], 1)
                    scores(0, c)
                pe.wait_ge(S["Rm"], c + 1)
                for h in range(HA):
                    last = mm(ps(1, n, 4, P)[:, h], U[c][0:n, h, 0:n], Rm[0:n, h], start=True, stop=True)
                last.then_inc(S["dl_full"], 1)
                if c == 0:
                    scores(0, 0)
                pe.wait_ge(S["dl"], c + 1)
                if c:
                    pe.wait_ge(S["oT"], c)
                for h in range(HA):
                    last = mm(ps(2, P, 4, n)[:, h], dl[0:n, h], PT[c][0:n, h, 0:n], start=True, stop=c == 0)
                    if c:
                        last = mm(ps(2, P, 4, n)[:, h], St[:, h], co[:, h, c0:c0 + n], start=False, stop=True)
                last.then_inc(S["oT_full"], 1)
                for h in range(HA):
                    last = mm(ps(3, P, 4, P)[:, h], Kr[c][0:n, h], dl[0:n, h], start=True, stop=True)
                last.then_inc(S["SU_full"], 1)
            pe.wait_ge(S["oT"], 3)
            pe.wait_ge(S["scan_S"], 3)
            for h in range(HF + 2):
                g = h - 2
                if g >= 0:
                    p_, t_, bk = pr[g % 2], pT[g % 2], bank[6]
                    pe.wait_ge(S["fnorm"], g + 1)
                    if g:
                        pe.wait_ge(S["fcopy"], g)
                    tr(bk[:, 0:128], p_[:, 0:128], ident[:, :])
                    tr(bk[:, 128:256], p_[:, 128:256], ident[:, :])
                    tr(bk[:, 272:400], p_[:, 256:384], ident[:, :])
                    tr(bk[:, 256:272], p_[0:16, 384:512], ident[0:16, 0:16])
                    tr(bk[:, 400:416], p_[0:16, 512:640], ident[0:16, 0:16])
                    tr(bk[0:16, 416:432], p_[0:16, 640:656], ident[0:16, 0:16]).then_inc(S["fT_full"], 1)
                if h < HF:
                    if h >= 3:
                        pe.wait_ge(S["fexp"], h - 2)
                    if h:
                        for qt in range(3):
                            scores(h, qt)
                if g >= 0:
                    pe.wait_ge(S["fcopy"], g + 1)
                    j, hp = g // 2, 64 * (g % 2)
                    if j:
                        pe.wait_ge(S["fout"], j)
                    ob = bank[7]
                    hs = slice(64 * g, 64 * g + 64)
                    mm(ob[hp:hp + 64, 0:NP], vr[:, 0, hs], t_[:, 0:NP], start=True, stop=False)
                    mm(ob[hp:hp + 64, P:NP], vr[:, 1, hs], t_[:, 272:416], start=False, stop=False)
                    last = mm(ob[hp:hp + 64, 256:NP], vr[0:16, 2, hs], t_[0:16, 416:432], start=False, stop=True)
                    if g % 2:
                        last.then_inc(S["fo_full"], 1)
            pe.wait_ge(S["fout"], 4)

            def states(b0, b1):
                for b in range(b0, b1):
                    for h in range(HA):
                        rhs = co[:, 0:8, NP + b].rearrange("p (e h) -> p h e", e=2)[:, h]
                        n = 2 * (4 * b + h)
                        last = mm(bank[7][:, n:n + 2], sS[:, 4 * b + h], rhs, start=True, stop=True)
                return last

            pe.wait_ge(S["ex_lf"], 1)
            flat = "p h b n -> p (h b n)"
            b0 = ps(0, P, 512)
            mm(b0, lows, lfc[:, :, :, :].rearrange(flat), start=True, stop=False)
            mm(b0, ones[:, :], rfx[:, :, :, :].rearrange(flat), start=False, stop=False)
            mm(b0.rearrange("p (x n) -> p x n", n=NPAGE), ones[0:NS, :],
               spread(ex8[:, 0:8, :].rearrange("p h b -> p (h b)"), 2, NPAGE), start=False, stop=True).then_inc(S["sbias_full"], 1)
            mm(bank[1][:, 0:192], ones[0:NS, :], ex8[:, :, :].rearrange("p x b -> p (x b)"), start=True, stop=True
               ).then_inc(S["sbc_full"], 1)
            states(0, 2)
            pe.wait_ge(S["m1"], 1)
            tr(bank[2][0:64, 0:P], m1, ident[:, :]).then_inc(S["m1T"], 1)
            states(2, 4)
            pe.wait_ge(S["mdiag"], 1)
            mm(bank[3][:, 0:64], ones[0:64, :], mdiag, start=True, stop=True).then_inc(S["mB"], 1)
            for c in range(4):
                last = tr(bank[4][:, 8 * c:8 * c + 8], vD[:, P * c:P * c + P], ident[0:NS, 0:NS])
            last.then_inc(S["vT_full"], 1)
            pe.wait_ge(S["qkprod"], 1)
            mm(bank[7][:, 256:288], ones[:, :], s32[:, 0].rearrange("p h b -> p (h b)"), start=True, stop=True)
            states(4, NS).then_inc(S["qSkS"], 1)
            pe.wait_ge(S["lsum"], 1)
            mm(bank[5][:, 0:64], ones[:, :], lsum, start=True, stop=True).then_inc(S["lB"], 1)
            for b in range(NS):
                pe.wait_ge(S["staged"], b + 1)
                for n in range(NPAGE):
                    slot = 2 * (b % 2) + n // 4
                    if n % 4 == 0:
                        pe.wait_ge(S[f"vslot{slot}_in"], (b // 2 + 1) * 64)
                    a = n % 2
                    last = mm(bank[6][64 * a:64 * a + 64, :], stage[b % 2][:, 64 * n:64 * n + 64], kc[:, slot, n % 4],
                              start=b == 0 and n < 2, stop=b == NS - 1 and n >= NPAGE - 2)
                    if n % 4 == 3:
                        last.then_inc(S[f"vslot{slot}_used"], 1)
                if b == 0:
                    pe.wait_ge(S["dT"], 1)
                    for h in range(HA):
                        tr(bank[2][0:NS, P * h:P * h + P], s32[:, 3, h], ident[:, :])
                        last = tr(bank[3][0:NS, P * h:P * h + P], co[:, 4 + h, NP:T], ident[:, :])
                    last.then_inc(S["dD_full"], 1)
                elif b <= HA:
                    h = b - 1
                    pe.wait_ge(S["Dx"], h + 1)
                    if h:
                        pe.wait_ge(S["sS_done"], h)
                    for q in range(2):
                        last = mm(ps(q, P, 512), dD[:, 1, P * h:P * h + P], Dx[:, 4 * q:4 * q + 4, :].rearrange("p b v -> p (b v)"),
                                  start=True, stop=True)
                    last.then_inc(S["outer"], 1)
                if b >= 4:
                    pe.wait_ge(S["osq"], b - 3)
                    mm(ps(4 + b % 2, P, T), ones[:, :], sq2, start=True, stop=True).then_inc(S["osum"], 1)
            pe.wait_ge(S["vsum"], 1)
            for c in range(4):
                last = mm(bank[2][:, 16 * c:16 * c + 16], vsum[:, P * c:P * c + P], ident2[:, 16 * c:16 * c + 16], start=True, stop=True)
            last.then_inc(S["picked"], 1)

        @block.vector
        def _(dve):
            me = Steps(dve, S["dve2"])
            tt, ts, stt, cp = nc.vector.tensor_tensor, nc.vector.tensor_scalar, nc.vector.scalar_tensor_tensor, nc.vector.tensor_copy
            red = nc.vector.tensor_reduce
            me.step(tt(lows, ones[:, :], tri[:, :], ALU.subtract))
            me.step(ts(nmask[:, :], tris[:, :], -1e30, None, ALU.mult))
            me.link(tt(iota_i[:, :], iota_i[:, :], part_i[:, :], ALU.bitwise_xor))
            me.step(cp(xorf, iota_i[:, :]))
            me.step(nc.vector.memset(mx[:, :, :], 0.0))
            me.link(nc.vector.memset(ls[:, :, :], 1.0))
            for c, (c0, n) in enumerate(CHUNKS):
                b0 = 4 * (c % 2)
                dve.wait_ge(S["prep_full"], c + 1)
                KK, QK, GB, G = ps(b0, n, 4, n), ps(b0 + 1, n, 4, n), ps(b0 + 2, P, 4, n), ps(b0 + 3, n, 4)
                me.link(cp(Gc[0:n, c], G))
                r_, d_ = raw[0:n, :, 0:n], dec[0:n, :, 0:n]
                dve.wait_ge(S["EGB"], c + 1)
                me.link(tt(r_, GB[0:n], spread(Gc[0:n, c], 2, n), ALU.subtract))
                ts(d_, r_, 0.0, None, ALU.max).then_inc(S["raw_pos"], 1)
                me.link(tt(kd[0:n, c], GB[0:n, :, n - 1], Gc[0:n, c], ALU.subtract))
                ts(kd[0:n, c], kd[0:n, c], 0.0, None, ALU.min).then_inc(S["kd_arg"], 1)
                ts(r_, r_, 0.0, None, ALU.min).then_inc(S["raw_neg"], 1)
                dve.wait_ge(S["decA"], c + 1)
                me.link(tt(d_, d_, KK, ALU.mult))
                me.link(tt(d_, d_, spread(lows[0:n, 0:n], 1, 4), ALU.mult))
                tt(Am[c][0:n], d_, spread(sm[0:n, c, 0:4], 2, n), ALU.mult).then_inc(S[f"A{c}_set"], 1)
                dve.wait_ge(S["decT"], c + 1)
                me.link(tt(r_, r_, QK, ALU.mult))
                tt(PT[c][0:n, :, 0:n], r_, spread(tri[0:n, 0:n], 1, 4), ALU.mult).then_inc(S["prep_used"], 1)
                tt(co[:, 0:4, c0:c0 + n], co[:, 0:4, c0:c0 + n], EGB[:, :, 0:n], ALU.mult).then_inc(S["qg_done"], 1)
                me.link(stt(nbe[0:n, c], nbe[0:n, c], -1.0, sm[0:n, c, 0:4], ALU.mult, ALU.mult))

            def off_blocks(c, n, lv):
                stt(Em[c][0:n], spread(xorf[0:n, 0:n], 1, 4), float(2 << lv), Am[c][0:n], ALU.is_lt, ALU.mult
                    ).then_inc(S[f"E{c}"], 1)

            for c, (c0, n) in enumerate(CHUNKS):
                dve.wait_ge(S[f"A{c}_set"], 1)
                off_blocks(c, n, 0)
            dve.wait_ge(S["cT_full"], 1)
            ts(ncT[:, :], bank[7][0:HF, P:P + NP], -1.0, None, ALU.mult).then_inc(S["ncT"], 1)
            for lv in range(7):
                for c, (c0, n) in enumerate(CHUNKS):
                    if lv + 1 < levels(c):
                        dve.wait_ge(S[f"A{c}"], lv + 1)
                        dve.wait_ge(S[f"M{c}"], lv + 1)
                        off_blocks(c, n, lv + 1)
                for c, (c0, n) in enumerate(CHUNKS):
                    if lv < levels(c):
                        dve.wait_ge(S[f"UU{c}"], lv + 1)
                        if lv + 1 < levels(c):
                            tt(Tm[c][0:n], Tm[c][0:n], tbank(c, n), ALU.subtract)
                        tt(U[c][0:n], U[c][0:n], ps([1, 5, 7][c], n, 4, n), ALU.subtract).then_inc(S[f"U{c}"], 1)
            dve.wait_ge(S["Kr_Vb"], 6)
            for c, (c0, n) in enumerate(CHUNKS):
                if c == 0:
                    cp(Rm[0:n], Vb[c][0:n]).then_inc(S["Rm"], 1)
                else:
                    dve.wait_ge(S["kS_full"], c)
                    for h in range(HA):
                        last = stt(Rm[0:n, h], ps(0, n, 4, P)[:, h], nbe[0:n, c, h:h + 1], Vb[c][0:n, h], ALU.mult, ALU.add)
                    last.then_inc(S["Rm"], 1)
                dve.wait_ge(S["SU_full"], c + 1)
                if c == 0:
                    cp(St[:, :, :], ps(3, P, 4, P)).then_inc(S["scan_S"], 1)
                else:
                    for h in range(HA):
                        last = stt(St[:, h], St[:, h], gend[:, c, h:h + 1], ps(3, P, 4, P)[:, h], ALU.mult, ALU.add)
                    last.then_inc(S["scan_S"], 1)
            tt(s32[:, 0], co[:, 0:4, NP:T], co[:, 4:8, NP:T], ALU.mult).then_inc(S["qkprod"], 1)
            me.link(nc.vector.memset(rfx[:, :, :, NPAGE - 1], 0.0))
            for n in range(NPAGE - 2, -1, -1):
                me.link(tt(rfx[:, :, :, n], rfx[:, :, :, n + 1], lfc[:, :, :, n + 1], ALU.add))
            me.link(tt(prod8, qD[:, :], kD[:, :], ALU.mult))
            me.link(red(dD[:, 0, 0:8], prod8.rearrange("p (h d) -> p h d", h=HF), AX.X, ALU.add))
            i8 = ident[0:NS, 0:NS]
            tt(ex8[:, 8:16, :], spread(dD[:, 0, 0:8], 2, NS), spread(i8, 1, 8), ALU.mult)
            tt(ex8[:, 16:20, :], spread(sm[0:NS, 3, 0:4], 2, NS), spread(i8, 1, 4), ALU.mult)
            dve.wait_ge(S["egr"], 1)
            tt(ex8[:, 20:24, :], spread(egr[:, :], 2, NS), spread(i8, 1, 4), ALU.mult)
            tt(ex8[:, 0:8, :], spread(sm[0:NS, 3, 8:16], 2, NS), spread(i8, 1, 8), ALU.mult).then_inc(S["ex_lf"], 1)
            for h in range(HF + 2):
                g = h - 1
                if 0 <= g < HF:
                    dve.wait_ge(S["fexp"], g + 1)
                    l_, p_ = ls[:, g % 2], pr[g % 2]
                    me.link(nc.vector.reciprocal(l_, l_))
                    ts(p_[:, 0:128], p_[:, 0:128], l_[:, 0:1], None, ALU.mult)
                    ts(p_[:, 128:384], p_[:, 128:384], l_[:, 1:2], None, ALU.mult)
                    ts(p_[0:16, 384:656], p_[0:16, 384:656], l_[0:16, 2:3], None, ALU.mult).then_inc(S["fnorm"], 1)
                if h < HF:
                    dve.wait_ge(S["fs_full"], h + 1)
                    bx, by = score_banks(h)
                    m_ = mx[:, h % 2]
                    red(m_[:, 0:1], bank[bx][:, 0:128], AX.X, ALU.max)
                    red(m_[:, 1:2], bank[bx][:, 128:384], AX.X, ALU.max)
                    me.link(red(m_[0:16, 2:3], bank[by][0:16, 0:272], AX.X, ALU.max))
                    ts(m_, m_, -1.0, None, ALU.mult).then_inc(S["fmax"], 1)
                if h >= 3 and h % 2:
                    j = (h - 2) // 2
                    dve.wait_ge(S["fo_full"], j + 1)
                    cp(qk[:, j, 0:NP], ps(7, P, NP)).then_inc(S["fout"], 1)
            for a in stage:
                me.step(nc.vector.memset(a, 0.0))
            me.step(tt(ident2, ident[:, 0:64], ident[:, 64:P], ALU.add))
            dve.wait_ge(S["sbias_full"], 1)
            me.link(tt(sc[:, :, :, :].rearrange("p h b n -> p (h b n)"), sc[:, :, :, :].rearrange("p h b n -> p (h b n)"),
                       ps(0, P, 512), ALU.add))
            red(m1, sc[:, :, :, :].rearrange("p h b n -> p (h b) n"), AX.X, ALU.max).then_inc(S["m1"], 1)
            dve.wait_ge(S["sbc_full"], 1)
            me.step(cp(snb, bank[1][:, 64:128]))
            me.link(cp(bge[:, :, :].rearrange("p x b -> p (x b)"), bank[1][:, 128:192]))
            dve.wait_ge(S["m1T"], 1)
            me.link(red(mcol, bank[2][0:64, 0:P], AX.X, ALU.max))
            ts(mdiag, ident[0:64, 0:64], mcol, None, ALU.mult).then_inc(S["mdiag"], 1)
            dve.wait_ge(S["mB"], 1)
            me.link(tt(mall, bank[3][:, 0:64], snb, ALU.max))
            tt(sc[:, :, :, :].rearrange("p h b n -> p (h b) n"), sc[:, :, :, :].rearrange("p h b n -> p (h b) n"),
               spread(mall, 2, NPAGE), ALU.subtract)
            tt(pn, snb, mall, ALU.subtract).then_inc(S["s_arg"], 1)
            dve.wait_ge(S["vT_full"], 1)
            me.link(cp(vT[:, :, :].rearrange("p c b -> p (c b)"), bank[4][:, 0:32]))
            def put_stage(b):
                if b >= 2:
                    dve.wait_ge(S[f"vslot{2 * (b % 2) + 1}_used"], b // 2)
                    me.step(nc.vector.memset(stage4[b % 2][:, :, :, b - 2], 0.0))
                cp(stage4[b % 2][:, :, :, b], sc[:, :, b].rearrange("p h n -> p n h")).then_inc(S["staged"], 1)

            dve.wait_ge(S["s_exp"], 1)
            put_stage(0)
            put_stage(1)
            red(lsum, sc[:, :, :, :].rearrange("p h b n -> p (h b) n"), AX.X, ALU.add).then_inc(S["lsum"], 1)
            dve.wait_ge(S["lB"], 1)
            me.link(tt(lrec, bank[5][:, 0:64], pn, ALU.add))
            me.link(nc.vector.reciprocal(lrec, lrec))

            dve.wait_ge(S["qSkS"], 1)
            X = bank[7][:, 0:64].rearrange("p (b h e) -> p e h b", h=4, e=2)
            beta, eg = bge[:, 0:4], bge[:, 4:8]
            me.link(tt(s32[:, 1], X[:, 1], eg, ALU.mult))
            me.link(tt(s32[:, 1], co[:, 8:12, NP:T], s32[:, 1], ALU.subtract))
            tt(s32[:, 3], s32[:, 1], beta, ALU.mult).then_inc(S["dT"], 1)
            dve.wait_ge(S["dT"], 1)
            me.step(tt(s32[:, 1], X[:, 0], eg, ALU.mult))
            me.link(tt(s32[:, 2], bank[7][:, 256:288].rearrange("p (h b) -> p h b", h=4), s32[:, 3], ALU.mult))
            me.link(tt(co[:, 8:12, NP:T], s32[:, 1], s32[:, 2], ALU.add))

            def rows_of_deltas(h):
                tt(Dx[:, :, :], spread(dD[:, 0, P * h:P * h + P], 1, NS), spread(i8, 2, P), ALU.mult).then_inc(S["Dx"], 1)

            dve.wait_ge(S["nga_in"], 16)
            for b in range(NS):
                if b + 2 < NS:
                    put_stage(b + 2)
                if b == 0:
                    dve.wait_ge(S["dD_full"], 1)
                    me.step(cp(dD[:, 0], bank[2][0:NS, :]))
                    me.link(cp(dD[:, 1], bank[3][0:NS, :]))
                    rows_of_deltas(0)
                elif b <= HA:
                    h = b - 1
                    dve.wait_ge(S["outer"], h + 1)
                    if h + 1 < HA:
                        rows_of_deltas(h + 1)
                    for n in range(NS):
                        s_ = sS[:, 4 * n + h]
                        last = stt(s_, s_, bge[:, 4 + h, n:n + 1], ps(n // 4, P, 4, P)[:, n % 4], ALU.mult, ALU.add)
                    last.then_inc(S["sS_done"], 1)
                if b >= 3:
                    c = b - 3
                    if c:
                        dve.wait_ge(S["orr"], c)
                        me.link(stt(co[:, 7 + c], co[:, 7 + c], nga[:, :], rr2, ALU.mult, ALU.mult))
                        tt(co[:, 7 + c], co[:, 7 + c], zs[:, c - 1], ALU.mult).then_inc(S["oa_done"], 1)
                    if c < 4:
                        tt(sq2, co[:, 8 + c], co[:, 8 + c], ALU.mult).then_inc(S["osq"], 1)
            dve.wait_ge(S["picked"], 1)
            for e in range(2):
                hs = slice(64 * e, 64 * e + 64)

                def heads(a):
                    return a[hs].rearrange("p (c e b) -> p e c b", c=4, e=2)[:, e]
                t_ = s32[hs, 4]
                me.link(tt(t_, heads(pn), vT[hs], ALU.mult))
                me.link(tt(t_, t_, heads(bank[2][:, 0:64]), ALU.add))
                me.link(tt(qk[hs, 0:4, NP:T], t_, heads(lrec), ALU.mult))

    blk2.close()
    if stop < 3:
        return
    S.renew()
    TILE = [P, P, 40]
    COLS = [(0, P), (P, P), (2 * P, 40)]
    blk3 = ctx.enter_context(ExitStack())
    mixT = sb("mixT", [P, KT, T], c=blk3)
    t2 = sb("t2", [P, 2, T], c=blk3)
    gffn = sb("gffn", [P, D], c=blk3)
    wr = sb("wr", [P, KT, NEXP], c=blk3)
    brt = sb("brt", [P, NEXP], c=blk3)
    ss3 = sb("ss3", [P, 4], c=blk3)
    mask = sb("mask", [P, 3, NEXP], c=blk3)
    rid_i = sb("rid_i", [P, 3], I32, c=blk3)
    valid = sb("valid", [P, 1], c=blk3)
    lg = sb("lg", [P, 3, NEXP], c=blk3)
    m8 = sb("m8", [P, 3, 8], c=blk3)
    ix8 = sb("ix8", [P, 3, 8], U32, c=blk3)
    idf = sb("idf", [P, 3, TOPK], c=blk3)
    oh4 = sb("oh4", [P, 3, TOPK, NEXP], c=blk3)
    wsum = sb("wsum", [P, 3], c=blk3)
    rank = sb("rank", [P, 3, NEXP], c=blk3)
    cnt = sb("cnt", [P, 2], c=blk3)
    pf = wg[:, 0:4, :]
    h2r = sg[:, :, :].rearrange("p a b -> p (a b)")[:, 0:3 * D].rearrange("p (t n) -> p t n", t=3)
    h2T = co[:, :, :].rearrange("p a b -> p (a b)")[:, 0:KT * 296].rearrange("p (k c) -> p k c", k=KT)

    W = {"gate": wg, "up": wu, "down": wd}
    halves = {"gate": lambda w, h: w.rearrange("o (p k) n -> p (o k) n", k=KT)[:, 4 * h:4 * h + 4],
              "down": lambda w, h: w[:, 512 * h:512 * h + 512].rearrange("o (p t) n -> p (o t) n", t=4)}
    halves["up"] = halves["gate"]

    def load_half(sp, name, e, h):
        sp.dma_start(W[name][:, 4 * h:4 * h + 4], halves[name](i["w_" + name][0, bass.ds(e, 1)], h)).then_inc(
            S[f"{name}{h}_in"], 16)

    def load_matrix(sp, name, e):
        for h in range(2):
            load_half(sp, name, e, h)

    with nc.Block() as block:

        @block.sync
        def _(sp):
            sp.dma_start(pf, i["p_f"][0].rearrange("(k p) n -> p k n", p=P)).then_inc(S["pf_in"], 16)
            sp.dma_start(wd[:, :, :], i["w_o"][0].rearrange("(k p) n -> p k n", p=P)).then_inc(S["wo_in"], 16)
            sp.dma_start(gffn[:, :], i["g_ffn"].to_broadcast([P, D])).then_inc(S["gffn_in"], 16)
            sp.dma_start(wr[:, :, :], i["w_router"][0].rearrange("(k p) n -> p k n", p=P)).then_inc(S["wr_in"], 16)
            sp.dma_start(brt[:, :], i["b_router"].to_broadcast([P, NEXP])).then_inc(S["wr_in"], 16)
            load_matrix(sp, "up", 0)
            sp.wait_ge(S["mixed"], 2 * KT)
            load_matrix(sp, "gate", 0)
            for t in range(3):
                sp.wait_ge(S["h2_rows"], t + 1)
                sp.dma_start(h_dram[P * t:P * t + TILE[t], :], h2r[0:TILE[t], t]).then_inc(S["h2_stored"], 16)
            load_matrix(sp, "down", 0)
            sp.wait_ge(S["h2_stored"], 48)

        @block.gpsimd
        def _(pool):
            nc.gpsimd.iota(iota_i[:, :], [[1, P]], 0, 0).then_inc(S["iota3"], 1)
            nc.gpsimd.iota(rid_i[:, :], [[P, 3]], 0, 1).then_inc(S["iota3"], 1)

        @block.scalar
        def _(act):
            me = Steps(act, S["act3"])
            nc.scalar.preload_act_table_set("natural_log_exp_and_others")
            for t in range(3):
                n = TILE[t]
                act.wait_ge(S["x_mid"], t + 1)
                me.link(nc.scalar.activation(h2r[0:n, t], xr[0:n, t], ACT.Square, accum_out=ss3[0:n, t:t + 1]))
                me.link(nc.scalar.activation(ss3[0:n, t:t + 1], ss3[0:n, t:t + 1], ACT.Ln, scale=1.0 / D, bias=epsb[0:n, :]))
                nc.scalar.activation(ss3[0:n, t:t + 1], ss3[0:n, t:t + 1], ACT.Exp, scale=-0.5).then_inc(S["rstd_m"], 1)
            act.wait_ge(S["w4_arg"], 1)
            nc.scalar.activation(w4[:, :, :], w4[:, :, :], ACT.Exp).then_inc(S["w4_exp"], 1)

        @block.tensor
        def _(pe):
            mm, tr = nc.tensor.matmul, nc.tensor.transpose
            for j in range(2 * KT):
                if j == KT:
                    pe.wait_ge(S["pf_in"], 16)
                if j >= 4:
                    pe.wait_ge(S["mixed"], j - 3)
                w, src = (pa, co[:, 8:12]) if j < KT else (pf, qk[:, 0:4])
                for k in range(4):
                    last = mm(ps(j % 4, P, T), w[:, k, P * (j % KT):P * (j % KT) + P], src[:, k], start=k == 0, stop=k == 3)
                last.then_inc(S["branch_full"], 1)

            def turned(t):
                n = TILE[t]
                pe.wait_ge(S["h2_rows"], t + 1)
                if t:
                    pe.wait_ge(S["h2T"], t)
                for k in range(KT):
                    last = tr(bank[k // 4][:, P * (k % 4):P * (k % 4) + n], h2r[0:n, t, P * k:P * k + P], ident[0:n, 0:n])
                last.then_inc(S["h2T_full"], 1)

            def logits(t):
                c0, n = COLS[t]
                pe.wait_ge(S["h2T"], t + 1)
                for k in range(KT):
                    last = mm(bank[2][0:n, NEXP * t:NEXP * t + NEXP], h2T[:, k, c0:c0 + n], wr[:, k], start=k == 0, stop=k == KT - 1)
                return last

            pe.wait_ge(S["mixed"], 2 * KT)
            pe.wait_ge(S["wo_in"], 16)
            for t in range(3):
                for half in range(2):
                    b = 4 + (2 * t + half) % 4
                    if t == 2:
                        pe.wait_ge(S["x_mid"], 1)
                    for k in range(KT):
                        w = wd[:, k, 512 * half:512 * half + 512]
                        for _, p0, c0, n in (ROWS[t:t + 1] if t < 2 else ROWS[2:]):
                            last = mm(bank[b][p0:p0 + n, :], mixT[:, k, c0:c0 + n], w, start=k == 0, stop=k == KT - 1)
                last.then_inc(S["wo_full"], 1)
                if t:
                    turned(t - 1)
            pe.wait_ge(S["wr_in"], 32)
            logits(0)
            turned(2)
            logits(1)
            logits(2).then_inc(S["logits"], 1)
            pe.wait_ge(S["mask"], 1)
            for t in range(3):
                for u in range(t + 1):
                    last = mm(bank[3][:, NEXP * t:NEXP * t + NEXP], (tris if u == t else ones)[:, :], mask[:, u], start=u == 0, stop=u == t)
            for u in range(3):
                last = mm(bank[3][:, 96:128], ones[:, :], mask[:, u], start=u == 0, stop=u == 2)
            last.then_inc(S["ranks"], 1)

        @block.vector
        def _(dve):
            me = Steps(dve, S["dve3"])
            tt, ts, stt, cp = nc.vector.tensor_tensor, nc.vector.tensor_scalar, nc.vector.scalar_tensor_tensor, nc.vector.tensor_copy
            red = nc.vector.tensor_reduce
            for j in range(KT):
                dve.wait_ge(S["branch_full"], j + 1)
                tt(mixT[:, j], ps(j % 4, P, T), sg[:, j], ALU.mult).then_inc(S["mixed"], 1)
            for j in range(KT):
                dve.wait_ge(S["branch_full"], KT + j + 1)
                me.link(tt(t2[:, j % 2], ps(j % 4, P, T), sg[:, 8 + j], ALU.mult))
                tt(mixT[:, j], mixT[:, j], t2[:, j % 2], ALU.add).then_inc(S["mixed"], 1)

            def x_mid(t):
                dve.wait_ge(S["wo_full"], t + 1)
                for half in range(2):
                    b = 4 + (2 * t + half) % 4
                    c = slice(512 * half, 512 * half + 512)
                    for _, p0, c0, n in (ROWS[t:t + 1] if t < 2 else ROWS[2:]):
                        last = tt(xr[p0:p0 + n, t, c], xr[p0:p0 + n, t, c], bank[b][p0:p0 + n, :], ALU.add)
                last.then_inc(S["x_mid"], 1)

            def rows(t):
                n = TILE[t]
                dve.wait_ge(S["rstd_m"], t + 1)
                stt(h2r[0:n, t], xr[0:n, t], ss3[0:n, t:t + 1], gffn[0:n, :], ALU.mult, ALU.mult).then_inc(S["h2_rows"], 1)

            def columns(t):
                c0, n = COLS[t]
                dve.wait_ge(S["h2T_full"], t + 1)
                for q in range(2):
                    last = cp(h2T[:, 4 * q:4 * q + 4, c0:c0 + n], ps(q, P, 4, P)[:, :, 0:n])
                last.then_inc(S["h2T"], 1)

            x_mid(0)
            dve.wait_ge(S["gffn_in"], 16)
            rows(0)
            x_mid(1)
            columns(0)
            rows(1)
            x_mid(2)
            columns(1)
            rows(2)
            columns(2)
            me.link(nc.vector.memset(valid[:, :], 0.0))
            me.step(nc.vector.memset(valid[0:16, :], 1.0))
            me.step(nc.vector.memset(valid[32:40, :], 1.0))
            me.step(nc.vector.memset(lg[:, :, :], 0.0))
            me.link(nc.vector.memset(m8[:, :, :], 0.0))
            dve.wait_ge(S["iota3"], 2)
            me.step(cp(iota64[:, :], iota_i[:, 0:SLOTS]))
            me.step(cp(dest[:, :, :, 0], spread(rid_i[:, :], 2, NEXP)))
            me.step(nc.vector.memset(hi64[0:64, :], 0.0))
            me.step(nc.vector.memset(hi64[64:P, :], 1.0))
            dve.wait_ge(S["logits"], 1)
            dve.wait_ge(S["wr_in"], 32)
            for t in range(3):
                n = TILE[t]
                me.step(tt(lg[0:n, t], bank[2][0:n, NEXP * t:NEXP * t + NEXP], brt[0:n, :], ALU.add))
            me.settle()
            for t in range(3):
                me.step(nc.vector.max(out=m8[:, t], in_=lg[:, t]))
            me.settle()
            for t in range(3):
                me.step(nc.vector.max_index(ix8[:, t], m8[:, t], lg[:, t]))
            tt(w4[:, :, :], m8[:, :, 0:TOPK], m8[:, :, 0:1].to_broadcast([P, 3, TOPK]), ALU.subtract).then_inc(S["w4_arg"], 1)
            me.settle()
            me.link(cp(idf[:, :, :], ix8[:, :, 0:TOPK]))
            me.link(ts(idf[:, 2], idf[:, 2], valid[:, :], None, ALU.mult))
            for t in range(3):
                me.step(tt(oh4[:, t], spread(iota64[:, 0:NEXP], 1, TOPK), spread(idf[:, t], 2, NEXP), ALU.is_equal))
            me.settle()
            me.link(red(mask[:, :, :], oh4[:, :, :, :].rearrange("p t k e -> p t e k"), AX.X, ALU.add))
            ts(mask[:, 2], mask[:, 2], valid[:, :], None, ALU.mult).then_inc(S["mask"], 1)
            dve.wait_ge(S["w4_exp"], 1)
            me.link(red(wsum[:, :], w4[:, :, :], AX.X, ALU.add))
            me.link(nc.vector.reciprocal(wsum[:, :], wsum[:, :]))
            me.step(tt(w4[:, :, :], w4[:, :, :], spread(wsum[:, :], 2, TOPK), ALU.mult))
            for t in range(3):
                me.step(tt(oh4[:, t], oh4[:, t], spread(iota64[:, 0:TOPK], 2, NEXP), ALU.mult))
            me.settle()
            me.link(red(lg[:, :, :], oh4[:, :, :, :].rearrange("p t k e -> p t e k"), AX.X, ALU.add))
            me.link(stt(lg[:, :, :], dest[:, :, :, 0], float(TOPK), lg[:, :, :], ALU.mult, ALU.add))
            me.link(ts(lg[:, :, :], lg[:, :, :], 1.0, 2.0, ALU.add, ALU.mult))
            me.link(tt(dest[:, :, :, 1], lg[:, :, :], mask[:, :, :], ALU.mult))
            dve.wait_ge(S["ranks"], 1)
            me.step(cp(rank[:, :, :], ps(3, P, 3, NEXP)))
            me.link(red(cnt[:, 0:1], bank[3][:, 96:128], AX.X, ALU.max))
            me.step(ts(cnt[:, 1:2], cnt[:, 0:1], float(SLOTS - 1), None, ALU.add))
            me.link(stt(code[:, :, :], rank[:, :, :], 1.0, mask[:, :, :], ALU.add, ALU.mult))
            me.step(ts(code[:, :, :], code[:, :, :], -1.0, None, ALU.add))
            me.link(cp(cnt_i[:, :], cnt[:, 1:2]))
            me.step(ts(cnt_i[:, :], cnt_i[:, :], 6, None, ALU.logical_shift_right))

    blk3.close()
    mix.close()
    if stop < 4:
        return
    blk4 = ctx.enter_context(ExitStack())
    oh = sb("oh", [P, 3, 2, SLOTS], c=blk4)
    idx = sb("idx", [P, 2], I32, c=blk4)
    idn = sb("idn", [P, 1], c=blk4)
    idy = sb("idy", [P, 1], I32, c=blk4)
    xg = sb("xg", [SLOTS, D], c=blk4)
    xT = sb("xT", [P, KT, SLOTS], c=blk4)
    g1 = sb("g1", [P, 512], c=blk4)
    sig = sb("sig", [P, 512], c=blk4)
    u1 = sb("u1", [P, 512], c=blk4)
    hT2 = sb("hT2", [P, 4, P], c=blk4)
    ysb = sb("ysb", [P, 512], c=blk4)
    brow = sb("brow", [1, 3, D], c=blk4)
    B = {"gate": brow[:, 0], "up": brow[:, 1], "down": brow[:, 2]}

    def turns(eng):
        return eng.value_load(cnt_i[0:1, 0:1], min_val=1, max_val=MAXPASS) * NEXP

    with nc.Block() as block:

        @block.sync
        def _(sp):
            for name in ("gate", "up", "down"):
                sp.dma_start(B[name], i["b_" + name][0, 0:1, :]).then_inc(S[f"{name}_b_in"], 16)
            with sp.Fori(0, turns(sp) - 1) as turn:
                for name in ("gate", "up", "down"):
                    e = (turn + 1) % NEXP
                    sp.wait_ge(S[f"{name}0_used"], turn + 1)
                    sp.dma_start(B[name], i["b_" + name][0, bass.ds(e, 1), :]).then_inc(S[f"{name}_b_in"], 16)
                    load_half(sp, name, e, 0)
                    sp.wait_ge(S[f"{name}_full"], turn + 1)
                    load_half(sp, name, e, 1)

        @block.gpsimd
        def _(pool):

            def gather(k):
                pool.wait_ge(S["idx"], k + 1)
                pool.sem_inc(S["xg_asked"], 1)
                nc.gpsimd.indirect_dma_start(
                    out=xg[:, :], out_offset=None, in_=h_dram,
                    in_offset=bass.IndirectOffsetOnAxis(ap=idx[0:SLOTS, 0:1], axis=0)).then_inc(S["xg_in"], 16)

            pool.wait_ge(S["h2_stored"], 48)
            gather(0)
            n = turns(pool)
            pool.dma_start(y_dram[0:1, 0, 0:SLOTS], ones[0:1, 0:SLOTS]).then_inc(S["y_stored"], 16)
            with pool.Fori(0, n) as turn:
                pool.wait_ge(S["xgT_full"], turn + 1)
                gather(turn + 1)
                pool.wait_ge(S["idy"], turn + 1)
                pool.wait_ge(S["down_evac"], turn + 1)
                pool.sem_inc(S["y_asked"], 1)
                nc.gpsimd.indirect_dma_start(
                    out=y_dram.rearrange("r h n -> (r h) n"), out_offset=bass.IndirectOffsetOnAxis(ap=idy[:, 0:1], axis=0),
                    in_=ysb[:, :], in_offset=None).then_inc(S["y_stored"], 16)
            pool.wait_ge(S["y_stored"], n * 16 + 16)
            pool.wait_ge(S["xg_in"], n * 16 + 16)

        @block.tensor
        def _(pe):
            mm, tr = nc.tensor.matmul, nc.tensor.transpose

            def lists(k, e):
                pe.wait_ge(S["oh"], k + 1)
                pe.wait_ge(S["idn"], k)
                for t in range(3):
                    n = TILE[t]
                    last = mm(bank[7][:, 0:2], oh[0:n, t].rearrange("p a s -> p (a s)"), dest[0:n, t, bass.ds(e, 1), :],
                              start=t == 0, stop=t == 2)
                last.then_inc(S["idx_full"], 1)

            def bias(turn, name, b):
                pe.wait_ge(S[f"{name}_b_in"], (turn + 1) * 16)
                for a in range(2):
                    mm(bank[b][64 * a:64 * a + 64, :], ones[0:1, 0:SLOTS], B[name][:, 512 * a:512 * a + 512], start=True, stop=False)

            def product(turn, name, b, lhs):
                for k in range(KT):
                    if k % 4 == 0:
                        pe.wait_ge(S[f"{name}{k // 4}_in"], (turn + 1) * 16)
                    for a in range(2):
                        last = mm(bank[b][64 * a:64 * a + 64, :], lhs(k), W[name][:, k, 512 * a:512 * a + 512],
                                  start=False, stop=k == KT - 1)
                    if k == 3:
                        last.then_inc(S[f"{name}0_used"], 1)
                last.then_inc(S[f"{name}_full"], 1)

            lists(0, 0)
            with pe.Fori(0, turns(pe)) as turn:
                pe.wait_ge(S["xg_in"], (turn + 1) * 16)
                bias(turn, "gate", 0)
                for k in range(KT):
                    last = tr(bank[6][:, SLOTS * k:SLOTS * k + SLOTS], xg[:, :].rearrange("s (p k) -> s k p", k=KT)[:, k],
                              ident[0:SLOTS, 0:SLOTS])
                last.then_inc(S["xgT_full"], 1)
                lists(turn + 1, (turn + 1) % NEXP)
                pe.wait_ge(S["xT"], turn + 1)
                product(turn, "gate", 0, lambda k: xT[:, k])
                bias(turn, "up", 1)
                product(turn, "up", 1, lambda k: xT[:, k])
                pe.wait_ge(S["h_act"], turn + 1)
                for t in range(4):
                    last = tr(bank[2][:, P * t:P * t + P], u1[:, :].rearrange("p (c t) -> p t c", t=4)[:, t], ident[:, :])
                last.then_inc(S["hT_full"], 1)
                bias(turn, "down", 3)
                pe.wait_ge(S["hT2"], turn + 1)
                product(turn, "down", 3, lambda k: hT2[:, k % 4, 64 * (k // 4):64 * (k // 4) + 64])

        @block.scalar
        def _(act):
            nc.scalar.preload_act_table(ACT.Sigmoid)
            with act.Fori(0, turns(act)) as turn:
                act.wait_ge(S["gate_evac"], turn + 1)
                nc.scalar.activation(sig[:, :], g1[:, :], ACT.Sigmoid, scale=1.702).then_inc(S["sig"], 1)
                act.wait_ge(S["hT_full"], turn + 1)
                nc.scalar.activation(hT2[:, :, :], ps(2, P, 4, P), ACT.Copy).then_inc(S["hT2"], 1)
                act.wait_ge(S["down_full"], turn + 1)
                act.wait_ge(S["y_stored"], turn * 16 + 16)
                nc.scalar.activation(ysb[:, :], ps(3, P, 512), ACT.Copy).then_inc(S["down_evac"], 1)

        @block.vector
        def _(dve):
            tt, ts, stt, cp = nc.vector.tensor_tensor, nc.vector.tensor_scalar, nc.vector.scalar_tensor_tensor, nc.vector.tensor_copy

            def onehot(k, e):
                dve.wait_ge(S["idx_full"], k)
                c_ = code[:, :, bass.ds(e, 1)]
                for a in range(2):
                    last = tt(oh[:, :, a], spread(iota64[:, :], 1, 3), c_.to_broadcast([P, 3, SLOTS]), ALU.is_equal)
                last.then_inc(S["oh"], 1)
                dve.wait_ge(S["oh"], k + 1)
                ts(c_, c_, -float(SLOTS), None, ALU.add).then_inc(S["code"], 1)

            def tokens(k):
                dve.wait_ge(S["idx_full"], k + 1)
                dve.wait_ge(S["xg_in"], k * 16)
                cp(idx[0:SLOTS, :], bank[7][0:SLOTS, 0:2]).then_inc(S["idx"], 1)

            def rows():
                cp(idn[:, :], bank[7][:, 1:2]).then_inc(S["idn"], 1)

            onehot(0, 0)
            tokens(0)
            rows()
            onehot(1, 1)
            with dve.Fori(0, turns(dve)) as turn:
                dve.wait_ge(S["xgT_full"], turn + 1)
                cp(xT[:, :, :], ps(6, P, KT, SLOTS)).then_inc(S["xT"], 1)
                tokens(turn + 1)
                dve.wait_ge(S["gate_full"], turn + 1)
                ts(g1[:, :], ps(0, P, 512), 7.0, None, ALU.min).then_inc(S["gate_evac"], 1)
                dve.wait_ge(S["sig"], turn + 1)
                tt(g1[:, :], g1[:, :], sig[:, :], ALU.mult).then_inc(S["gs"], 1)
                dve.wait_ge(S["up_full"], turn + 1)
                ts(u1[:, :], ps(1, P, 512), -7.0, 7.0, ALU.max, ALU.min).then_inc(S["up_evac"], 1)
                dve.wait_ge(S["up_evac"], turn + 1)
                dve.wait_ge(S["gs"], turn + 1)
                stt(u1[:, :], u1[:, :], 1.0, g1[:, :], ALU.add, ALU.mult).then_inc(S["h_act"], 1)
                dve.wait_ge(S["y_stored"], turn * 16 + 16)
                dve.wait_ge(S["idn"], turn + 1)
                tt(idy[:, :], idn[:, :], hi64[:, :], ALU.add).then_inc(S["idy"], 1)
                dve.wait_ge(S["idy"], turn + 1)
                rows()
                onehot(turn + 2, (turn + 2) % NEXP)

    if stop < 5:
        return
    yk = [w[:, 0:4, :] for w in (wg, wu, wd)]

    with nc.Block() as block:

        @block.vector
        def _(dve):
            for t in (0, 2, 1):
                n = TILE[t]
                for k in range(TOPK):
                    dve.wait_ge(S["y2_in"] if t == 2 else S[f"y{t}{k}_in"], 32 if t == 2 else 16)
                    nc.vector.scalar_tensor_tensor(xr[0:n, t], yk[t][0:n, k], w4[0:n, t, k:k + 1], xr[0:n, t], ALU.mult, ALU.add
                                                   ).then_inc(S[f"out{t}"], 1)
                    dve.wait_ge(S[f"out{t}"], k + 1)

        @block.sync
        def _(sp):
            yrows = y_dram[1:, :, :].rearrange("(r k) h n -> r k (h n)", k=TOPK)
            for k in range(TOPK):
                sp.dma_start(yk[0][:, k], yrows[0:P, k]).then_inc(S[f"y0{k}_in"], 16)
            for _, p0, c0, m in ROWS[2:]:
                sp.dma_start(yk[2][p0:p0 + m], yrows[2 * P + p0:2 * P + p0 + m]).then_inc(S["y2_in"], 16)
            for k in range(TOPK):
                sp.dma_start(yk[1][:, k], yrows[P:2 * P, k]).then_inc(S[f"y1{k}_in"], 16)
            sp.wait_ge(S["out0"], TOPK)
            sp.dma_start(o["y_prompt"][0, 0:P - NMETA, :], xr[NMETA:P, 0]).then_inc(S["y_out"], 16)
            sp.wait_ge(S["out2"], TOPK)
            sp.dma_start(o["y_sample"].rearrange("b t d -> (b t) d"), xr[32:32 + NS, 2]).then_inc(S["y_out"], 16)
            sp.dma_start(o["y_prompt"][0, 2 * P - NMETA:, :], xr[0:NMETA, 2]).then_inc(S["y_out"], 16)
            sp.wait_ge(S["out1"], TOPK)
            sp.dma_start(o["y_prompt"][0, P - NMETA:2 * P - NMETA, :], xr[:, 1]).then_inc(S["y_out"], 16)
            sp.wait_ge(S["y_out"], 64)


_INS = ["x_prompt", "x_sample", "cache_k", "cache_v", "cache_logf", "state_delta", "state_conv", "page_table",
        "meta_tokens", "g_mix", "w_in", "conv_w", "a_log", "dt_bias", "norm_a", "qn_g", "kn_g", "b_forget",
        "p_a", "p_f", "w_o", "g_ffn", "w_router", "b_router", "w_gate", "b_gate", "w_up", "b_up", "w_down", "b_down"]
_OUTS = {
    "y_prompt": (1, 256, 1024), "y_sample": (8, 1, 1024),
    "k_prompt": (1, 1, 272, 8, 64), "v_prompt": (1, 1, 272, 8, 64), "logf_prompt": (1, 1, 272, 8),
    "k_sample": (1, 8, 1, 8, 64), "v_sample": (1, 8, 1, 8, 64), "logf_sample": (1, 8, 1, 8),
    "delta_prompt": (1, 1, 4, 128, 128), "delta_sample": (1, 8, 4, 128, 128),
    "conv_prompt": (1, 1, 3, 1536), "conv_sample": (1, 8, 3, 1536),
}


def kernel(**inputs):
    import numpy as np
    import concourse.bacc as bacc
    from concourse.bass_utils import run_bass_kernel_spmd

    nc = bacc.Bacc("TRN2", target_bir_lowering=False, num_devices=1)
    arrays, ins, outs = {}, {}, {}
    for name in _INS:
        a = np.ascontiguousarray(inputs[name])
        arrays[f"in_{name}"] = a
        ins[name] = nc.dram_tensor(f"in_{name}", a.shape, mybir.dt.from_np(a.dtype), kind="ExternalInput").ap()
    for name, shape in _OUTS.items():
        outs[name] = nc.dram_tensor(f"out_{name}", shape, F32, kind="ExternalOutput").ap()
    program(nc, ins, outs)
    r = run_bass_kernel_spmd(nc, [arrays], core_ids=[0])
    return tuple(r.results[0][f"out_{name}"] for name in _OUTS)
```
